# Optimizing a Trainium2 kernel written in Bass

```python
import math
import jax, jax.numpy as jnp
from jax import lax
import numpy as np

D_MODEL = 1024
BATCH = 1
SEQ = 512
DEPTH = 2

CHUNK = 64
N_MIXERS = 4
Q_BLOCK = 128
EPS = 1e-6
NEG_INF = -1e30
CONV_WIDTH = 3
MLA_HEADS = 16
MLA_Q_LORA = 256
MLA_KV_LORA = 256
MLA_NOPE = 64
MLA_ROPE = 32
MLA_V = 64
ROPE_THETA = 10000.0
GMLP_BLOCK = 128
GMLP_HALF = 2 * D_MODEL
GMLP_GROUPS = 8
GMLP_GC = GMLP_HALF // GMLP_GROUPS
SWA_WINDOW = 128
WIN_CHUNKS = SWA_WINDOW // CHUNK
WIN_KEYS = WIN_CHUNKS * CHUNK
SWA_Q_HEADS = 16
SWA_KV_HEADS = 4
SWA_GROUP = SWA_Q_HEADS // SWA_KV_HEADS
SWA_HD = 64
REL_BUCKETS = 32
REL_MAX_DIST = 128
FFN_HIDDEN = ((8 * D_MODEL + 3 * 256 - 1) // (3 * 256)) * 256

kernel_name = "hybrid_chunk_causal_interleaved_trunk"

def n_layers_of(m):
    return len(range(m, DEPTH, N_MIXERS))

def rms_norm(x, g):
    xf = x.astype(jnp.float32)
    y = xf * lax.rsqrt(jnp.mean(xf * xf, axis=-1, keepdims=True) + EPS)
    return (y * g.astype(jnp.float32)).astype(x.dtype)

def layer_norm(x, g, b):
    xf = x.astype(jnp.float32)
    mu = jnp.mean(xf, axis=-1, keepdims=True)
    xc = xf - mu
    y = xc * lax.rsqrt(jnp.mean(xc * xc, axis=-1, keepdims=True) + EPS)
    return (y * g.astype(jnp.float32) + b.astype(jnp.float32)).astype(x.dtype)

def rope_tables(seq, dim):
    inv = ROPE_THETA ** (-jnp.arange(0, dim, 2, dtype=jnp.float32) / dim)
    ang = jnp.arange(seq, dtype=jnp.float32)[:, None] * inv[None, :]
    return jnp.cos(ang), jnp.sin(ang)

def apply_rope(x, cos, sin):
    x1, x2 = jnp.split(x.astype(jnp.float32), 2, axis=-1)
    return jnp.concatenate([x1 * cos - x2 * sin, x2 * cos + x1 * sin], axis=-1).astype(x.dtype)

def t5_bucket(rel):
    half = REL_BUCKETS // 2
    max_exact = half // 2
    ret = jnp.where(rel > 0, half, 0)
    n = jnp.abs(rel)
    nf = jnp.maximum(n, 1).astype(jnp.float32)
    large = max_exact + (jnp.log(nf / max_exact) / math.log(REL_MAX_DIST / max_exact)
                         * (half - max_exact)).astype(jnp.int32)
    large = jnp.minimum(large, half - 1)
    return ret + jnp.where(n < max_exact, n, large)

def short_conv_mixer(h, w_in, conv_w, w_out):
    b_gate, c_gate, xt = jnp.split(h @ w_in, 3, axis=-1)
    z = c_gate * xt
    conv = lax.conv_general_dilated(
        z, conv_w[:, None, :], window_strides=(1,), padding=[(CONV_WIDTH - 1, 0)],
        dimension_numbers=('NWC', 'WIO', 'NWC'), feature_group_count=D_MODEL)
    return (b_gate * conv) @ w_out

def mla_mixer(h, w_dq, q_g, w_uq, w_dkv, kv_g, w_ukv, w_o):
    bsz, s, _ = h.shape
    cq = rms_norm(h @ w_dq, q_g)
    q = (cq @ w_uq).reshape(bsz, s, MLA_HEADS, MLA_NOPE + MLA_ROPE)
    q_nope, q_rope = q[..., :MLA_NOPE], q[..., MLA_NOPE:]
    ckv = h @ w_dkv
    c_kv = rms_norm(ckv[..., :MLA_KV_LORA], kv_g)
    kv = (c_kv @ w_ukv).reshape(bsz, s, MLA_HEADS, MLA_NOPE + MLA_V)
    k_nope, v = kv[..., :MLA_NOPE], kv[..., MLA_NOPE:]
    cos, sin = rope_tables(s, MLA_ROPE)
    q_rope = apply_rope(q_rope, cos[:, None, :], sin[:, None, :])
    k_rope = apply_rope(ckv[..., MLA_KV_LORA:], cos, sin)
    scale = (MLA_NOPE + MLA_ROPE) ** -0.5
    pos = jnp.arange(s)
    outs = []
    for j in range(s // Q_BLOCK):
        q0, q1 = j * Q_BLOCK, (j + 1) * Q_BLOCK
        kend = q1
        logits = (jnp.einsum('bqhd,bkhd->bhqk', q_nope[:, q0:q1], k_nope[:, :kend])
                  + jnp.einsum('bqhr,bkr->bhqk', q_rope[:, q0:q1], k_rope[:, :kend]))
        logits = logits.astype(jnp.float32) * scale
        mask = (pos[None, :kend] // CHUNK) <= (pos[q0:q1, None] // CHUNK)
        logits = jnp.where(mask[None, None], logits, NEG_INF)
        p = jax.nn.softmax(logits, axis=-1).astype(v.dtype)
        outs.append(jnp.einsum('bhqk,bkhd->bqhd', p, v[:, :kend]))
    o = jnp.concatenate(outs, axis=1).reshape(bsz, s, MLA_HEADS * MLA_V)
    return o @ w_o

def gmlp_mixer(h, w_in, ln_g, ln_b, w_s, b_s, w_out):
    bsz, s, _ = h.shape
    uv = jax.nn.gelu(h @ w_in)
    u, v = uv[..., :GMLP_HALF], uv[..., GMLP_HALF:]
    v = layer_norm(v, ln_g, ln_b)
    v = v.reshape(bsz, s // GMLP_BLOCK, GMLP_BLOCK, GMLP_GROUPS, GMLP_GC)
    t = jnp.arange(GMLP_BLOCK)
    mask = (t[None, :] // CHUNK) <= (t[:, None] // CHUNK)
    ws = jnp.where(mask[None], w_s, jnp.zeros_like(w_s))
    z = jnp.einsum('gts,bnsgc->bntgc', ws, v) + b_s.T[None, None, :, :, None]
    return (u * z.reshape(bsz, s, GMLP_HALF)) @ w_out

def window_keys(t):
    nc = t.shape[1]
    tp = jnp.concatenate([jnp.zeros_like(t[:, :WIN_CHUNKS - 1]), t], axis=1)
    return jnp.concatenate([tp[:, w:w + nc] for w in range(WIN_CHUNKS)], axis=2)

def swa_sink_mixer(h, w_qkv, sinks, w_o, rel_bias):
    bsz, s, _ = h.shape
    nc = s // CHUNK
    qkv = h @ w_qkv
    qw, kvw = SWA_Q_HEADS * SWA_HD, SWA_KV_HEADS * SWA_HD
    q = qkv[..., :qw].reshape(bsz, nc, CHUNK, SWA_KV_HEADS, SWA_GROUP, SWA_HD)
    k = qkv[..., qw:qw + kvw].reshape(bsz, nc, CHUNK, SWA_KV_HEADS, SWA_HD)
    v = qkv[..., qw + kvw:].reshape(bsz, nc, CHUNK, SWA_KV_HEADS, SWA_HD)
    kw, vw = window_keys(k), window_keys(v)
    logits = jnp.einsum('bcqhgd,bckhd->bchgqk', q, kw).astype(jnp.float32) * SWA_HD ** -0.5
    qi = jnp.arange(CHUNK)
    kj = jnp.arange(WIN_KEYS)
    rel = kj[None, :] - (WIN_CHUNKS - 1) * CHUNK - qi[:, None]
    bias = rel_bias[t5_bucket(rel)].astype(jnp.float32)
    bias = bias.transpose(2, 0, 1).reshape(SWA_KV_HEADS, SWA_GROUP, CHUNK, WIN_KEYS)
    logits = logits + bias[None, None]
    key_chunk = jnp.arange(nc)[:, None] - (WIN_CHUNKS - 1) + kj[None, :] // CHUNK
    valid = key_chunk >= 0
    logits = jnp.where(valid[None, :, None, None, None, :], logits, NEG_INF)
    sink = jnp.broadcast_to(
        sinks.astype(jnp.float32).reshape(SWA_KV_HEADS, SWA_GROUP)[None, None, :, :, None, None],
        logits.shape[:-1] + (1,))
    p = jax.nn.softmax(jnp.concatenate([logits, sink], axis=-1), axis=-1)[..., :-1]
    o = jnp.einsum('bchgqk,bckhd->bcqhgd', p.astype(vw.dtype), vw)
    return o.reshape(bsz, s, qw) @ w_o

def swiglu_ffn(h, w_gate, w_up, w_down):
    return (jax.nn.silu(h @ w_gate) * (h @ w_up)) @ w_down

def setup_inputs(seed: int = 0) -> dict:
    key = jax.random.key(seed)
    ks = iter(jax.random.split(key, 40))
    f32 = jnp.float32

    def w(shape, fan_in):
        return jax.random.normal(next(ks), shape, f32) * fan_in ** -0.5

    def gain(shape):
        return 1.0 + 0.05 * jax.random.normal(next(ks), shape, f32)

    na, nb, ncm, nd = (n_layers_of(m) for m in range(N_MIXERS))
    d = D_MODEL
    return {
        "x": jax.random.normal(next(ks), (BATCH, SEQ, d), f32),
        "norm_mix_g": gain((DEPTH, d)),
        "norm_ffn_g": gain((DEPTH, d)),
        "ffn_w_gate": w((DEPTH, d, FFN_HIDDEN), d),
        "ffn_w_up": w((DEPTH, d, FFN_HIDDEN), d),
        "ffn_w_down": w((DEPTH, FFN_HIDDEN, d), FFN_HIDDEN),
        "final_norm_g": gain((d,)),
        "rel_bias": 0.5 * jax.random.normal(next(ks), (REL_BUCKETS, SWA_Q_HEADS), f32),
        "conv_w_in": w((na, d, 3 * d), d),
        "conv_w": w((na, CONV_WIDTH, d), CONV_WIDTH),
        "conv_w_out": w((na, d, d), d),
        "mla_w_dq": w((nb, d, MLA_Q_LORA), d),
        "mla_q_norm_g": gain((nb, MLA_Q_LORA)),
        "mla_w_uq": w((nb, MLA_Q_LORA, MLA_HEADS * (MLA_NOPE + MLA_ROPE)), MLA_Q_LORA),
        "mla_w_dkv": w((nb, d, MLA_KV_LORA + MLA_ROPE), d),
        "mla_kv_norm_g": gain((nb, MLA_KV_LORA)),
        "mla_w_ukv": w((nb, MLA_KV_LORA, MLA_HEADS * (MLA_NOPE + MLA_V)), MLA_KV_LORA),
        "mla_w_o": w((nb, MLA_HEADS * MLA_V, d), MLA_HEADS * MLA_V),
        "gmlp_w_in": w((ncm, d, 2 * GMLP_HALF), d),
        "gmlp_ln_g": gain((ncm, GMLP_HALF)),
        "gmlp_ln_b": 0.02 * jax.random.normal(next(ks), (ncm, GMLP_HALF), f32),
        "gmlp_w_s": w((ncm, GMLP_GROUPS, GMLP_BLOCK, GMLP_BLOCK), GMLP_BLOCK),
        "gmlp_b_s": gain((ncm, GMLP_GROUPS, GMLP_BLOCK)),
        "gmlp_w_out": w((ncm, GMLP_HALF, d), GMLP_HALF),
        "swa_w_qkv": w((nd, d, (SWA_Q_HEADS + 2 * SWA_KV_HEADS) * SWA_HD), d),
        "swa_sinks": jax.random.normal(next(ks), (nd, SWA_Q_HEADS), f32),
        "swa_w_o": w((nd, SWA_Q_HEADS * SWA_HD, d), SWA_Q_HEADS * SWA_HD),
    }

def reference(x, norm_mix_g, norm_ffn_g, ffn_w_gate, ffn_w_up, ffn_w_down, final_norm_g,
              rel_bias, conv_w_in, conv_w, conv_w_out, mla_w_dq, mla_q_norm_g, mla_w_uq,
              mla_w_dkv, mla_kv_norm_g, mla_w_ukv, mla_w_o, gmlp_w_in, gmlp_ln_g, gmlp_ln_b,
              gmlp_w_s, gmlp_b_s, gmlp_w_out, swa_w_qkv, swa_sinks, swa_w_o):
    for i in range(DEPTH):
        m, j = i % N_MIXERS, i // N_MIXERS
        h = rms_norm(x, norm_mix_g[i])
        if m == 0:
            y = short_conv_mixer(h, conv_w_in[j], conv_w[j], conv_w_out[j])
        elif m == 1:
            y = mla_mixer(h, mla_w_dq[j], mla_q_norm_g[j], mla_w_uq[j], mla_w_dkv[j],
                          mla_kv_norm_g[j], mla_w_ukv[j], mla_w_o[j])
        elif m == 2:
            y = gmlp_mixer(h, gmlp_w_in[j], gmlp_ln_g[j], gmlp_ln_b[j], gmlp_w_s[j],
                           gmlp_b_s[j], gmlp_w_out[j])
        else:
            y = swa_sink_mixer(h, swa_w_qkv[j], swa_sinks[j], swa_w_o[j], rel_bias)
        x = x + y
        h = rms_norm(x, norm_ffn_g[i])
        x = x + swiglu_ffn(h, ffn_w_gate[i], ffn_w_up[i], ffn_w_down[i])
    return rms_norm(x, final_norm_g)


_drawn_inputs = setup_inputs


def setup_inputs(seed=0):
    import zlib

    import numpy as np

    out = dict(_drawn_inputs(seed))
    spreads = {}
    factors = {'mla_q_norm_g': 8.0, 'mla_kv_norm_g': 8.0}
    for name, (base, spread) in spreads.items():
        noise = np.random.default_rng([zlib.crc32(name.encode()), seed]).standard_normal(out[name].shape)
        drawn = base * np.exp(spread * noise) if base else spread * noise
        out[name] = __import__('jax').numpy.asarray(drawn.astype(out[name].dtype))
    for name, factor in factors.items():
        out[name] = (out[name] * factor).astype(out[name].dtype)
    return out
```

```python
from contextlib import ExitStack

import concourse.bass as bass
from concourse import mybir

F32 = mybir.dt.float32
F32R = mybir.dt.float32r
ACT = mybir.ActivationFunctionType
ALU = mybir.AluOpType
ds = bass.ds

P = 128
EPS = 1e-6
TILE_BANKS = 4
STAT_BANK = 7


def make_plan(n_hidden):
    shape = {
        "conv_in": (3, 8, [0, 1, 2], 3, [0, 1, 2]),
        "conv_out": (4, 2, [0, 1, 2, 3], 4, [0, 1, 2, 3]),
        "ffn0": (4, n_hidden // 2, [0, 1, 2, 3], 4, [0, 1, 2, 3]),
        "down0": (8, 4, [0, 1, 2, 3] * 2, 2, [0, 1]),
        "latent": (5, 1, [0, 1, 2, 3, 0], 5, [0, 1, 2, 3, 0]),
        "kv_up": (4, 1, [2, 3, 0, 1], 0, []),
        "q_up": (1, 8, [2], 0, []),
        "mla_out": (4, 2, [0, 1, 2, 3], 4, [0, 1, 2, 3]),
        "ffn1": (4, n_hidden // 2, [0, 1, 2, 3], 4, [0, 1, 2, 3]),
        "down1": (8, 4, [0, 1, 2, 3] * 2, 2, [0, 1]),
    }
    plan = {"shape": shape, "unit0": {}, "tile0": {"load": 0}, "home": []}
    slots, prev_unit, nth = [], [], []
    last, count = {}, {}
    banks = [t % TILE_BANKS for t in range(8)]
    for name, (ub, n, unit_slots, tb, tile_banks) in shape.items():
        plan["unit0"][name] = len(slots)
        plan["tile0"][name] = len(banks)
        for i in range(n):
            for u in range(ub):
                s, v = unit_slots[u], len(slots)
                slots.append(s)
                prev_unit.append(last.get(s))
                count[s] = count.get(s, 0) + 1
                nth.append(count[s])
                last[s] = v
                plan["home"].append((name, i, u))
            banks += tile_banks
    prev_tile, seen = [], {}
    for t, b in enumerate(banks):
        prev_tile.append(seen.get(b))
        seen[b] = t
    after, trigger = {}, -1
    for w, p in enumerate(prev_unit):
        trigger = max(trigger, -1 if p is None else p)
        after.setdefault(trigger, []).append(w)
    plan.update(slots=slots, prev_unit=prev_unit, nth=nth, prev_tile=prev_tile, after=after,
                units=len(slots), tiles=len(banks))
    return plan


def trunk_kernel(nc, w, consts, out):
    x_dram = w["x"].rearrange("b s d -> (b s) d")
    out_dram = out.rearrange("b s d -> (b s) d")
    S, D = x_dram.shape
    F = w["ffn_w_gate"].shape[2]
    DC = D // P
    FC = F // P
    TB = S // P
    HEADS, NOPE, ROPE, VD = 16, 64, 32, 64
    QK = NOPE + ROPE
    HALF = ROPE // 2
    LORA = w["mla_w_dq"].shape[2]
    LC = LORA // P
    SCALE = float(QK) ** -0.5
    PAIRS = HEADS // 2
    PAIR_SRC = 2 * QK
    assert (S, D, DC, TB, LC) == (512, 1024, 8, 4, 2) and FC % 2 == 0

    plan = make_plan(FC)
    U0, T0, shape = plan["unit0"], plan["tile0"], plan["shape"]
    quarter = [FC // 4 + (q < FC % 4) for q in range(4)]
    DOWN = [(sum(quarter[:q]), quarter[q]) for q in range(4)]

    rows = {}
    at = 0
    for name, n in (("mix0", DC), ("mix1", DC), ("ffn0", DC), ("ffn1", DC), ("final", DC),
                    ("tap0", DC), ("tap1", DC), ("tap2", DC), ("q_norm", LC), ("kv_norm", LC)):
        rows[name] = at
        at += n
    G_ROWS = at

    L_OFF = [P * j * (j + 1) // 2 for j in range(TB)]
    L_COLS = L_OFF[-1] + TB * P
    PT_OFF = {0: 0, 1: 512, 3: 896, 2: 1024}

    with ExitStack() as ctx:
        cursor = [0]
        ARENA = 207 * 1024
        arena = ctx.enter_context(nc.sbuf_tensor("arena", [P, ARENA // 4], F32))
        base = nc.sbuf_base - ARENA

        def place(name, dims, dt, offset=None):
            size = 4
            for n in dims[1:]:
                size *= n
            size = -(-size // 32) * 32
            if offset is None:
                offset = cursor[0]
                cursor[0] += size
            assert offset + size <= ARENA
            return nc.alloc_sbuf_tensor_at(name, dims, dt, offset=base + offset), offset, offset + size

        xT, _, _ = place("xT", [P, DC, S], F32)
        xg_hi, XG, _ = place("xg_hi", [P, DC, S], F32R)
        xg_lo, _, XG_END = place("xg_lo", [P, DC, S], F32R)
        hid_hi, HID, _ = place("hid_hi", [P, FC, S], F32R)
        hid_lo, HL, HID_END = place("hid_lo", [P, FC, S], F32R)
        wgt_hi, _, _ = place("wgt_hi", [P, 4, 1024], F32R)
        wgt_lo, _, _ = place("wgt_lo", [P, 4, 1024], F32R)
        raw, _, _ = place("raw", [P, 4, 1024], F32)
        inv, _, _ = place("inv", [P, S], F32)
        sq_sum, _, _ = place("sq_sum", [P, S], F32)
        sq, SQ, _ = place("sq", [P, S], F32)
        root, _, _ = place("root", [P, S], F32, SQ)
        ident_t, _, _ = place("ident", [P, P], F32)
        ident = ident_t[:, :]
        ones, _, _ = place("ones", [P, P], F32)
        gain, _, _ = place("gain", [P, G_ROWS], F32)
        small, _, _ = place("small", [P, 64], F32)
        _, TMP, _ = place("tmp_region", [P, 5 * S + 2], F32)
        c_r, _, e = place("c_r", [P, S], F32, TMP)
        x_r, _, e = place("x_r", [P, S], F32, e)
        z, _, e = place("z", [P, S + 2], F32, e)
        cv, _, e = place("cv", [P, S], F32, e)
        y, _, e = place("y", [P, S], F32, e)
        gate_r, _, e = place("gate_r", [P, S], F32, TMP)
        up_r, _, e = place("up_r", [P, S], F32, e)
        act, _, e = place("act", [P, S], F32, e)
        h, _, e = place("h", [P, S], F32, e)
        q_T, _, e = place("q_T", [P, 2, S], F32, TMP)
        rope_s, _, e = place("rope_s", [P, S], F32, e)
        k_rope, _, e = place("k_rope", [P, S], F32, e)
        inv_lat, _, e = place("inv_lat", [P, S], F32, e)
        x_nat, _, _ = place("x_nat", [P, TB, D], F32, HID)
        gain_rows, _, _ = place("gain_rows", [P, P], F32, HL)
        LAT = DC
        FREE_HI, FREE_LO = HID + (LAT + 2 * LC) * S * 4, HL + (LAT + 2 * LC) * S * 4
        k_T, _, e = place("k_T", [QK, HEADS, S], F32, XG)
        assert e <= XG_END
        v_nat, _, e = place("v_nat", [P, TB, HEADS * VD], F32, FREE_HI)
        v_head, _, e = place("v_head", [P, 2, TB, VD], F32, e)
        mask, _, e = place("mask", [P, S], F32, e)
        assert e <= HL
        prob, _, e = place("prob", [P, 2, L_COLS], F32, FREE_LO)
        c_kv, _, e2 = place("c_kv", [P, LC, S], F32, e)
        c_q, _, e2 = place("c_q", [P, LC, S], F32, e2)
        rope, _, e2 = place("rope", [P, S], F32, e2)
        assert e2 <= HID_END
        prob_T, _, e = place("prob_T", [P, 1, L_COLS], F32, e)
        prob_T2, _, e3 = place("prob_T2", [P, 1, L_COLS], F32, cursor[0])
        cursor[0] = e3
        prob_Ts = [prob_T, prob_T2]
        assert e <= HID_END
        o_nat, _, e = place("o_nat", [P, TB, D], F32, XG)
        o_chunk, _, e = place("o_chunk", [P, 2, S], F32, TMP)

        mx, neg_mx, sums, rec = (small[:, 8 * n:8 * n + 8].rearrange("p (b j) -> p b j", b=2) for n in range(4))
        root_c, inv_c = small[:, 32:32 + TB], small[:, 40:40 + TB]

        ps = ctx.enter_context(nc.psum_tensor("ps", [P, 8, 512], F32))

        def sem(name):
            return ctx.enter_context(nc.semaphore(name))

        ident_in, tables_in, gain_in = sem("ident_in"), sem("tables_in"), sem("gain_in")
        x_in = [sem(f"x_in{c}") for c in range(4)]
        raw_in = [sem(f"raw_in{s}") for s in range(4)]
        w_hi, w_lo, w_used = sem("w_hi"), sem("w_lo"), sem("w_used")
        ones_set, z_pad, gain_turned, gain_ready = sem("ones_set"), sem("z_pad"), sem("gain_turned"), sem("gain_ready")
        x_turned = sem("x_turned")
        tile_free = sem("tile_free")
        x_hi, x_lo = sem("x_hi"), sem("x_lo")
        sq_zero, sq_new, sq_added = sem("sq_zero"), sem("sq_new"), sem("sq_added")
        stat_done, root_done, inv_done = sem("stat_done"), sem("root_done"), sem("inv_done")
        conv_step, y_new, y_hi, y_lo = sem("conv_step"), sem("y_new"), sem("y_hi"), sem("y_lo")
        act_done, h_new, h_hi, h_lo = sem("act_done"), sem("h_new"), sem("h_hi"), sem("h_lo")
        rope_step, k_rope_done = sem("rope_step"), sem("k_rope_done")
        lat_sq, lat_sum, lat_scaled = sem("lat_sq"), sem("lat_sum"), sem("lat_scaled")
        lat_hi, lat_lo = sem("lat_hi"), sem("lat_lo")
        k_prod, k_out, v_prod, v_out = sem("k_prod"), sem("k_out"), sem("v_prod"), sem("v_out")
        k_rope_set = sem("k_rope_set")
        q_prod, q_nope, q_rope, q_step = sem("q_prod"), sem("q_nope"), sem("q_rope"), sem("q_step")
        s_prod, s_read, mx_neg, exp_done = sem("s_prod"), sem("s_read"), sem("mx_neg"), sem("exp_done")
        rec_done, p_ready, p_turned = sem("rec_done"), sem("p_ready"), sem("p_turned")
        pt_dve, pt_act, v_ready, pv_done = sem("pt_dve"), sem("pt_act"), sem("v_ready"), sem("pv_done")
        o_hi, o_lo = sem("o_hi"), sem("o_lo")
        out_scaled, out_turned, out_nat, stored = (sem("out_scaled"), sem("out_turned"),
                                                              sem("out_nat"), sem("stored"))
        out_final = [sem("out_final_even"), sem("out_final_odd")]

        passed = {e.engine: sem(f"passed_{n}") for n, e in (("sp", nc.sync), ("pool", nc.gpsimd), ("dve", nc.vector))}

        def wait(eng, semaphore, value):
            if isinstance(value, int) and value <= 0:
                return
            eng.wait_ge(semaphore, value)

        def wait_apart(eng, semaphore, value):
            wait(eng, semaphore, value)
            if not isinstance(value, int):
                eng.sem_inc(passed[eng.engine], 1)

        def chunked(m):
            return m.rearrange("(c p) n -> p c n", p=P)

        conv_in, conv_out = chunked(w["conv_w_in"][0]), chunked(w["conv_w_out"][0])
        w_dq, w_uq = chunked(w["mla_w_dq"][0]), chunked(w["mla_w_uq"][0])
        w_dkv, w_ukv, w_o = chunked(w["mla_w_dkv"][0]), chunked(w["mla_w_ukv"][0]), chunked(w["mla_w_o"][0])
        gates = [chunked(w["ffn_w_gate"][l]) for l in range(2)]
        ups = [chunked(w["ffn_w_up"][l]) for l in range(2)]
        downs = [chunked(w["ffn_w_down"][l]) for l in range(2)]

        def source(name, i, u):
            if name == "conv_in":
                return conv_in[:, :, ds(i * P + (1, 2, 0)[u] * D, P)], DC, P
            if name in ("conv_out", "mla_out"):
                m = conv_out if name == "conv_out" else w_o
                return m[:, :, ds(i * (4 * P) + u * P, P)], DC, P
            if name.startswith("ffn"):
                m = (gates, ups)[u % 2][int(name[-1])]
                return m[:, :, ds(i * (2 * P) + (u // 2) * P, P)], DC, P
            if name.startswith("down"):
                c0, n = DOWN[u % 4]
                return downs[int(name[-1])][:, c0:c0 + n, ds(i * (2 * P) + (u // 4) * P, P)], n, P
            if name == "latent":
                m, c0, n = ((w_dkv, 0, P), (w_dkv, P, P), (w_dkv, LORA + ROPE - QK, QK), (w_dq, 0, P), (w_dq, P, P))[u]
                return m[:, :, c0:c0 + n], DC, n
            if name == "kv_up":
                return w_ukv[:, :, u * 512:(u + 1) * 512], LC, 512
            return w_uq[:, :, ds(i * PAIR_SRC, PAIR_SRC)], LC, PAIR_SRC

        def unit_numbers(name, i, u):
            ub, n, slots, _, _ = shape[name]
            if isinstance(i, int):
                v = U0[name] + ub * i + u
                return v, plan["slots"][v], plan["prev_unit"][v], plan["nth"][v]
            used = len(set(slots))
            v1 = U0[name] + ub + u
            per_body = ub // used
            return (i * ub + (U0[name] + u), slots[u], i * ub + (plan["prev_unit"][v1] - ub),
                    i * per_body + (plan["nth"][v1] - per_body))

        def load_unit(eng, name, i, u):
            v, s, prev, _ = unit_numbers(name, i, u)
            src, n, width = source(name, i, u)
            if prev is not None:
                wait_apart(eng, w_lo, prev + 1)
            dst = raw[:, s, 0:n * width].rearrange("p (c n) -> p c n", c=n)
            eng.dma_start(dst, src).then_inc(raw_in[s], 16)

        def split_parts(name, s, n, width, part):
            dst, src = part[:, s, :], raw[:, s, 0:n * width]
            if name == "q_up" or width == QK:
                heads = width // QK
                d = dst[:, 0:n * heads * P].rearrange("p (c m) -> p c m", m=P)
                r = src.rearrange("p (c m) -> p c m", m=QK)
                return [(d[:, :, 0:QK], r), (d[:, :, QK:QK + HALF], r[:, :, NOPE + HALF:QK]),
                        (d[:, :, QK + HALF:P], r[:, :, NOPE:NOPE + HALF])]
            if name == "kv_up":
                r = src.rearrange("p (g m) -> p g m", m=2 * NOPE)
                return [(dst[:, o * 512:(o + 1) * 512].rearrange("p (g m) -> p g m", m=NOPE),
                         r[:, :, o * NOPE:(o + 1) * NOPE]) for o in range(2)]
            return [(dst[:, 0:n * width], src)]

        def unit_hi(eng, name, i, u):
            v, s, prev, nth = unit_numbers(name, i, u)
            _, n, width = source(name, i, u)
            eng.wait_ge(raw_in[s], nth * 16)
            if prev is not None:
                wait(eng, w_used, prev + 1)
            for dst, src in split_parts(name, s, n, width, wgt_hi):
                ins = nc.scalar.activation(dst, src, ACT.Copy)
            ins.then_inc(w_hi, 1)

        def unit_lo(eng, name, i, u):
            v, s, prev, nth = unit_numbers(name, i, u)
            _, n, width = source(name, i, u)
            wait(eng, w_hi, v + 1)
            for (dst, src), (hi, _) in zip(split_parts(name, s, n, width, wgt_lo),
                                           split_parts(name, s, n, width, wgt_hi)):
                ins = nc.vector.tensor_tensor(dst, src, hi.bitcast(F32), ALU.subtract)
            ins.then_inc(w_lo, 1)

        def prepare(eng, make, name, i, u):
            ub, n, slots, _, _ = shape[name]
            if isinstance(i, int):
                for v in plan["after"].get(U0[name] + ub * i + u, []):
                    make(eng, *plan["home"][v])
                return
            ahead = u + len(set(slots))
            make(eng, name, i + ahead // ub, ahead % ub)

        def product(acc, wh, wl, xh, xl, first, last):
            nc.tensor.matmul(acc, wh, xh, start=first, stop=False)
            nc.tensor.matmul(acc, wh, xl, start=False, stop=False)
            return nc.tensor.matmul(acc, wl, xh, start=False, stop=last)

        def tile_wait(eng, name, i, t):
            _, _, _, tb, banks = shape[name]
            if isinstance(i, int):
                prev = plan["prev_tile"][T0[name] + tb * i + t]
                if prev is not None:
                    eng.wait_ge(tile_free, prev + 1)
            else:
                wait(eng, tile_free, i * tb + (plan["prev_tile"][T0[name] + tb + t] - tb + 1))

        def chunk_products(name, i, u, ks, ready, ready0):
            pe = nc.tensor
            v, s, _, _ = unit_numbers(name, i, u)
            if ks[0] == 0:
                tile_wait(pe, name, i, u)
                wait(pe, w_lo, v + 1)
            hi, lo = (xg_hi, xg_lo) if ready is x_lo else (hid_hi, hid_lo)
            acc = ps[:, shape[name][4][u], :]
            for k in ks:
                if isinstance(i, int) and i == 0 and u == 0:
                    pe.wait_ge(ready, ready0 + k + 1)
                col = slice(k * P, k * P + P)
                ins = product(acc, wgt_hi[:, s, col], wgt_lo[:, s, col], hi[:, k, :], lo[:, k, :],
                              k == 0, k == DC - 1)
            if ks[-1] == DC - 1:
                ins.then_inc(w_used, 1)

        early, late, every = list(range(DC - 1)), [DC - 1], list(range(DC))

        def first_two(name, ready, ready0, stat=None):
            chunk_products(name, 0, 0, early, ready, ready0)
            chunk_products(name, 0, 1, early[:2], ready, ready0)
            if stat is not None:
                statistic(sq_added, stat)
            chunk_products(name, 0, 1, early[2:], ready, ready0)
            chunk_products(name, 0, 0, late, ready, ready0)
            chunk_products(name, 0, 1, late, ready, ready0)

        stats = [0]

        def statistic(ready, count):
            pe = nc.tensor
            pe.wait_ge(ready, count)
            if stats[0]:
                pe.wait_ge(root_done, stats[0])
            stats[0] += 1
            nc.tensor.matmul(ps[:, STAT_BANK, :], ones[:, :], sq_sum[:, :], start=True, stop=True).then_inc(stat_done, 1)


        def make_root(eng, n, width):
            eng.wait_ge(stat_done, n + 1)
            if n:
                eng.wait_ge(inv_done, n)
            nc.scalar.activation(root[:, :], ps[:, STAT_BANK, :], ACT.Sqrt, scale=1.0 / width,
                                 bias=small[:, 48:49]).then_inc(root_done, 1)

        def make_inv(eng, n, to=inv):
            eng.wait_ge(root_done, n + 1)
            nc.vector.reciprocal(to[:, :], root[:, :]).then_inc(inv_done, 1)
            eng.wait_ge(inv_done, n + 1)

        block = ctx.enter_context(nc.Block())

        @block.sync
        def _(sp):
            half = D // 4
            sp.dma_start(ident, consts[:, 0:P]).then_inc(ident_in, 16)
            for c in range(0, 4, 2):
                sp.dma_start(x_nat[:, :, c * half:(c + 1) * half],
                             x_dram.rearrange("(t p) d -> p t d", p=P)[:, :, c * half:(c + 1) * half]).then_inc(x_in[c], 16)
            for name in shape:
                ub, n = shape[name][0:2]
                for u in range(ub):
                    load_unit(sp, name, 0, u)
                if n > 1:
                    with sp.Fori(1, n) as i:
                        for u in range(ub):
                            load_unit(sp, name, i, u)
            for t in range(TB):
                sp.wait_ge(out_final[t % 2], t // 2 + 1)
                sp.dma_start(out_dram[t * P:(t + 1) * P, :], o_nat[:, t, :]).then_inc(stored, 16)
            sp.wait_ge(stored, 16 * TB)

        def latents(pool):
            pool.wait_ge(w_used, U0["latent"])
            pool.dma_start(mask[:, :], consts[:, P:P + S]).then_inc(tables_in, 16)
            pool.dma_start(rope[:, :], consts[:, P + S:P + 2 * S]).then_inc(tables_in, 16)
            for k, c in enumerate((c_kv, c_q)):
                pool.wait_ge(tile_free, T0["latent"] + (LC if k == 0 else LC + 1 + LC))
                pool.wait_ge(stat_done, 3 + k)
                pool.wait_ge(inv_done, 3 + k)
                nc.gpsimd.tensor_tensor(sq_sum[:, :], c[:, 0, :], c[:, 0, :], ALU.mult).then_inc(lat_sq, 1)
                nc.gpsimd.tensor_tensor(sq[:, :], c[:, 1, :], c[:, 1, :], ALU.mult).then_inc(lat_sq, 1)
                pool.wait_ge(lat_sq, 2 * k + 2)
                nc.gpsimd.tensor_tensor(sq_sum[:, :], sq_sum[:, :], sq[:, :], ALU.add).then_inc(lat_sum, 1)
            pool.wait_ge(k_rope_done, 1)
            pool.wait_ge(lat_sum, 2)
            pool.wait_ge(w_used, U0["latent"] + 5)
            for hd in range(HEADS):
                ins = nc.gpsimd.tensor_copy(k_T[NOPE:QK, hd, :], k_rope[NOPE:QK, :])
            ins.then_inc(k_rope_set, 1)

            def v_slice(hd, par):
                wait(pool, pv_done, hd - 1)
                nc.gpsimd.tensor_copy(v_head[:, par, :, :], v_nat[:, :, ds(hd * VD, VD)]).then_inc(v_ready, 1)

            def add_rope(hd, par):
                wait(pool, q_step, 2 * hd + 2)
                nc.gpsimd.tensor_tensor(q_T[NOPE:QK, par, :], q_T[NOPE:QK, par, :], rope_s[NOPE:QK, :],
                                        ALU.add).then_inc(q_rope, 1)

            pool.wait_ge(k_rope_set, 1)
            for par in range(2):
                add_rope(par, par)
            pool.wait_ge(v_out, 2 * TB)

            def heads(i, ahead=True):
                for par in range(2):
                    hd = 2 * i + par
                    wait(pool, q_rope, hd + (2 if ahead else 0))
                    v_slice(hd, par)
                    if ahead:
                        wait(pool, v_ready, hd + 1)
                        add_rope(hd + 2, par)

            heads(0)
            with pool.Fori(1, PAIRS - 1) as i:
                heads(i)
            pool.wait_ge(q_rope, HEADS)
            heads(PAIRS - 1, ahead=False)

        @block.gpsimd
        def _(pool):
            nc.gpsimd.memset(ones[:, :], 1.0).then_inc(ones_set, 1)
            nc.gpsimd.memset(small[:, :], EPS).then_inc(ones_set, 1)
            nc.gpsimd.memset(z[:, 0:2], 0.0).then_inc(z_pad, 1)

            def clear_sum(n):
                if n:
                    pool.wait_ge(stat_done, stat_of[n])
                nc.gpsimd.memset(sq_sum[:, :], 0.0).then_inc(sq_zero, 1)

            def add_square(n, m, tile):
                wait(pool, tile_free, tile + 1)
                wait(pool, sq_added, m + n * DC)
                nc.gpsimd.tensor_tensor(sq[:, :], xT[:, ds(m, 1), :].rearrange("p a s -> p (a s)"),
                                        xT[:, ds(m, 1), :].rearrange("p a s -> p (a s)"), ALU.mult).then_inc(sq_new, 1)
                wait(pool, sq_new, m + (n * DC + 1))
                pool.wait_ge(sq_zero, n + 1)
                nc.gpsimd.tensor_tensor(sq_sum[:, :], sq_sum[:, :], sq[:, :], ALU.add).then_inc(sq_added, 1)

            stat_of = {0: 0, 1: 1, 2: 2, 3: 5, 4: 6}
            clear_sum(0)
            for m in range(DC):
                add_square(0, m, T0["load"] + m)
            for n, name in ((1, "conv_out"), (2, "down0"), (3, "mla_out"), (4, "down1")):
                clear_sum(n)
                with pool.Fori(0, DC) as m:
                    add_square(n, m, m + T0[name])
                if n == 2:
                    latents(pool)

        @block.scalar
        def _(sc):
            half = D // 4

            def load_gains(row, g):
                n = g.shape[0]
                sc.dma_start(gain_rows[row:row + n, :], g).then_inc(gain_in, 16)

            load_gains(rows["mix0"], w["norm_mix_g"].rearrange("l (r c) -> (l r) c", c=P))
            for c in range(1, 4, 2):
                sc.dma_start(x_nat[:, :, c * half:(c + 1) * half],
                             x_dram.rearrange("(t p) d -> p t d", p=P)[:, :, c * half:(c + 1) * half]).then_inc(x_in[c], 16)
            load_gains(rows["ffn0"], w["norm_ffn_g"].rearrange("l (r c) -> (l r) c", c=P))
            load_gains(rows["final"], w["final_norm_g"].rearrange("(r c) -> r c", c=P))
            load_gains(rows["tap0"], w["conv_w"].rearrange("a t (r c) -> (a t r) c", c=P))
            load_gains(rows["q_norm"], w["mla_q_norm_g"].rearrange("a (r c) -> (a r) c", c=P))
            load_gains(rows["kv_norm"], w["mla_kv_norm_g"].rearrange("a (r c) -> (a r) c", c=P))
            for v in range(2):
                unit_hi(sc, *plan["home"][v])
            sc.wait_ge(gain_ready, 1)
            sc.wait_ge(ones_set, 2)

            def chunk(t, m):
                return t[:, ds(m, 1), :].rearrange("p a s -> p (a s)")

            def gain_hi(m, tile, g):
                wait(sc, tile_free, tile + 1)
                nc.scalar.activation(chunk(xg_hi, m), chunk(xT, m), ACT.Copy,
                                     scale=gain[:, ds(m + rows[g], 1)]).then_inc(x_hi, 1)

            for m in range(DC):
                gain_hi(m, T0["load"] + m, "mix0")
            unit_hi(sc, *plan["home"][2])
            make_root(sc, 0, D)

            def conv_body(i):
                prepare(sc, unit_hi, "conv_in", i, 0)
                prepare(sc, unit_hi, "conv_in", i, 1)
                wait(sc, y_new, i + 1)
                nc.scalar.activation(chunk(hid_hi, i), y[:, :], ACT.Copy).then_inc(y_hi, 1)
                prepare(sc, unit_hi, "conv_in", i, 2)

            with sc.Fori(0, DC - 1) as i:
                conv_body(i)
            conv_body(DC - 1)

            def out_body(name, i, g):
                for u in range(4):
                    gain_hi(4 * i + u, i * 4 + (T0[name] + u), g)
                    prepare(sc, unit_hi, name, i, u)

            out_body("conv_out", 0, "ffn0")
            out_body("conv_out", 1, "ffn0")

            def ffn(l, n_root):
                name = f"ffn{l}"
                make_root(sc, n_root, D)

                def body(i):
                    for t in range(2):
                        n = 2 * i + (t + l * FC)
                        wait(sc, tile_free, i * 4 + (T0[name] + 2 * t + 1))
                        nc.scalar.activation(act[:, :], gate_r[:, :], ACT.Silu).then_inc(act_done, 1)
                        prepare(sc, unit_hi, name, i, 2 * t)
                        prepare(sc, unit_hi, name, i, 2 * t + 1)
                        wait(sc, h_new, n + 1)
                        nc.scalar.activation(chunk(hid_hi, 2 * i + t), h[:, :], ACT.Copy).then_inc(h_hi, 1)

                with sc.Fori(0, FC // 2 - 1) as i:
                    body(i)
                body(FC // 2 - 1)

            ffn(0, 1)

            def down0_body(i):
                for u in range(8):
                    if u % 4 == 3:
                        m = u // 4
                        gain_hi(2 * i + m, i * 2 + (T0["down0"] + m), "mix1")
                    prepare(sc, unit_hi, "down0", i, u)

            with sc.Fori(0, 3) as i:
                down0_body(i)
            down0_body(3)

            prepare(sc, unit_hi, "latent", 0, 0)
            prepare(sc, unit_hi, "latent", 0, 1)
            make_root(sc, 2, D)
            prepare(sc, unit_hi, "latent", 0, 2)

            def latent_hi(k, g):
                for c in range(LC):
                    n = LC * k + c
                    sc.wait_ge(lat_scaled, n + 1)
                    src = (c_kv, c_q)[k][:, c, :]
                    nc.scalar.activation(hid_hi[:, LAT + n, :], src, ACT.Copy,
                                         scale=gain[:, rows[g] + c:rows[g] + c + 1]).then_inc(lat_hi, 1)

            make_root(sc, 3, LORA)
            latent_hi(0, "kv_norm")
            prepare(sc, unit_hi, "latent", 0, 3)
            prepare(sc, unit_hi, "latent", 0, 4)

            def k_copy(n):
                sc.wait_ge(k_prod, n + 1)
                for par in range(2):
                    ins = nc.scalar.activation(k_T[0:NOPE, 2 * n + par, :], ps[64 * par:64 * par + NOPE, n % 4, :], ACT.Copy)
                ins.then_inc(k_out, 1)

            for n in range(4):
                k_copy(n)
            make_root(sc, 4, LORA)
            latent_hi(1, "q_norm")
            for u in range(4):
                prepare(sc, unit_hi, "kv_up", 0, u)
            for n in range(4, PAIRS):
                k_copy(n)

            def exponentials(hd, par):
                wait(sc, mx_neg, hd + 1)
                for j in range(TB):
                    blk = prob[:, par, L_OFF[j]:L_OFF[j] + (j + 1) * P]
                    ins = nc.scalar.activation(blk, blk, ACT.Exp, bias=neg_mx[:, par, j:j + 1], scale=SCALE,
                                               accum_out=sums[:, par, j:j + 1])
                ins.then_inc(exp_done, 1)

            def turned_copy(hd, par):
                wait(sc, p_turned, 3 * hd + 2)
                wait(sc, pv_done, hd - 1)
                nc.scalar.activation(prob_Ts[par][:, 0, 1024:1280], ps[:, 5, 0:256], ACT.Copy)
                wait(sc, p_turned, 3 * hd + 3)
                nc.scalar.activation(prob_Ts[par][:, 0, 512:1024], ps[:, 4, :], ACT.Copy).then_inc(pt_act, 1)

            def head_out(pair):
                wait(sc, pv_done, 2 * pair + 2)
                nc.scalar.activation(chunk(hid_hi, pair), ps[:, 6, :], ACT.Copy).then_inc(o_hi, 1)

            def q_copy(hd, par):
                wait(sc, q_prod, hd + 1)
                nc.scalar.activation(q_T[0:NOPE, par, :], ps[0:NOPE, 7, :], ACT.Copy).then_inc(q_nope, 1)

            q_copy(0, 0)
            q_copy(1, 1)
            prepare(sc, unit_hi, "q_up", 0, 0)

            def attend(i, first=False, ahead=True, prep=True):
                for par in range(2):
                    exponentials(2 * i + par, par)
                    if not (first and par == 0):
                        turned_copy(2 * i + (par - 1), 1 - par)
                    if ahead:
                        q_copy(2 * i + (2 + par), par)
                if not first:
                    head_out(i - 1)
                if prep:
                    unit_hi(sc, "q_up", i + 2, 0)

            attend(0, first=True)
            attend(1)
            with sc.Fori(2, PAIRS - 2) as i:
                attend(i)
            attend(PAIRS - 2, prep=False)
            for v in range(U0["mla_out"], U0["mla_out"] + 4):
                unit_hi(sc, *plan["home"][v])
            attend(PAIRS - 1, ahead=False, prep=False)
            turned_copy(HEADS - 1, 1)
            head_out(PAIRS - 1)

            out_body("mla_out", 0, "ffn1")
            out_body("mla_out", 1, "ffn1")
            ffn(1, 5)

            def down1_body(i):
                for u in range(8):
                    if u % 4 == 3:
                        m = 2 * i + u // 4
                        wait(sc, tile_free, i * 2 + (T0["down1"] + u // 4 + 1))
                        wait(sc, out_turned, m - 1)
                        nc.scalar.activation(o_chunk[:, u // 4, :], chunk(xT, m), ACT.Copy,
                                             scale=gain[:, ds(m + rows["final"], 1)]).then_inc(out_scaled, 1)
                    prepare(sc, unit_hi, "down1", i, u)

            down1_body(0)
            with sc.Fori(1, 3) as i:
                down1_body(i)
            down1_body(3)
            sc.wait_ge(stat_done, 7)
            nc.scalar.activation(root_c, ps[:, STAT_BANK, 0:TB], ACT.Sqrt, scale=1.0 / D,
                                 bias=small[:, 48:49]).then_inc(root_done, 1)
            sc.wait_ge(inv_done, 7)
            sc.wait_ge(out_nat, DC)
            for t in range(1, TB, 2):
                nc.scalar.activation(o_nat[:, t, :], o_nat[:, t, :], ACT.Copy, scale=inv_c[:, t:t + 1]).then_inc(out_final[1], 1)

        @block.vector
        def _(ve):
            def chunk(t, m):
                return t[:, ds(m, 1), :].rearrange("p a s -> p (a s)")

            ve.wait_ge(gain_turned, 1)
            nc.vector.tensor_copy(gain[:, :], ps[:, 4, 0:G_ROWS]).then_inc(gain_ready, 1)
            ve.wait_ge(gain_ready, 1)
            unit_lo(ve, *plan["home"][0])
            unit_lo(ve, *plan["home"][1])

            def gain_lo(m, count, g):
                wait(ve, x_hi, count + 1)
                nc.vector.scalar_tensor_tensor(chunk(xg_lo, m), chunk(xT, m), gain[:, ds(m + rows[g], 1)],
                                               chunk(xg_hi, m).bitcast(F32), ALU.mult, ALU.subtract).then_inc(x_lo, 1)

            for m in range(DC + 1):
                if m < DC:
                    ve.wait_ge(x_turned, m + 1)
                    nc.vector.tensor_copy(xT[:, m, :], ps[:, m % TILE_BANKS, :]).then_inc(tile_free, 1)
                if m:
                    gain_lo(m - 1, m - 1, "mix0")
            unit_lo(ve, *plan["home"][2])
            make_inv(ve, 0)
            ve.wait_ge(z_pad, 1)

            def conv_body(i):
                unit = i * 3 + U0["conv_in"]
                step = 4 * i
                wait(ve, w_used, unit + 1)
                nc.vector.tensor_tensor(c_r[:, :], ps[:, 0, :], inv[:, :], ALU.mult).then_inc(tile_free, 1)
                prepare(ve, unit_lo, "conv_in", i, 0)
                wait(ve, w_used, unit + 2)
                nc.vector.tensor_tensor(x_r[:, :], ps[:, 1, :], inv[:, :], ALU.mult).then_inc(tile_free, 1)
                wait(ve, tile_free, i * 3 + (T0["conv_in"] + 2))
                nc.vector.tensor_tensor(z[:, 2:S + 2], c_r[:, :], x_r[:, :], ALU.mult).then_inc(conv_step, 1)
                wait(ve, conv_step, step + 1)
                nc.vector.tensor_scalar(cv[:, :], z[:, 2:S + 2], gain[:, ds(i + rows["tap2"], 1)], None,
                                        ALU.mult).then_inc(conv_step, 1)
                wait(ve, conv_step, step + 2)
                nc.vector.scalar_tensor_tensor(x_r[:, :], z[:, 1:S + 1], gain[:, ds(i + rows["tap1"], 1)], cv[:, :],
                                               ALU.mult, ALU.add).then_inc(conv_step, 1)
                wait(ve, conv_step, step + 3)
                nc.vector.scalar_tensor_tensor(cv[:, :], z[:, 0:S], gain[:, ds(i + rows["tap0"], 1)], x_r[:, :],
                                               ALU.mult, ALU.add).then_inc(conv_step, 1)
                prepare(ve, unit_lo, "conv_in", i, 1)
                wait(ve, w_used, unit + 3)
                nc.vector.tensor_tensor(c_r[:, :], ps[:, 2, :], inv[:, :], ALU.mult).then_inc(tile_free, 1)
                wait(ve, tile_free, i * 3 + (T0["conv_in"] + 3))
                wait(ve, conv_step, step + 4)
                nc.vector.tensor_tensor(y[:, :], c_r[:, :], cv[:, :], ALU.mult).then_inc(y_new, 1)
                wait(ve, y_hi, i + 1)
                nc.vector.tensor_tensor(chunk(hid_lo, i), y[:, :], chunk(hid_hi, i).bitcast(F32),
                                        ALU.subtract).then_inc(y_lo, 1)
                prepare(ve, unit_lo, "conv_in", i, 2)

            with ve.Fori(0, DC - 1) as i:
                conv_body(i)
            conv_body(DC - 1)

            def residual(m, bank, used):
                wait(ve, w_used, used)
                nc.vector.tensor_tensor(chunk(xT, m), ps[:, bank, :], chunk(xT, m), ALU.add).then_inc(tile_free, 1)

            def out_body(name, i, g, norm):
                for u in range(4):
                    m = 4 * i + u
                    residual(m, u, i * 4 + (U0[name] + u + 1))
                    wait(ve, tile_free, i * 4 + (T0[name] + u + 1))
                    gain_lo(m, m + norm * DC, g)
                    prepare(ve, unit_lo, name, i, u)

            out_body("conv_out", 0, "ffn0", 1)
            out_body("conv_out", 1, "ffn0", 1)

            def ffn(l, n_inv):
                name = f"ffn{l}"
                make_inv(ve, n_inv)

                def body(i):
                    for t in range(2):
                        n = 2 * i + (t + l * FC)
                        used, tile = i * 4 + (U0[name] + 2 * t), i * 4 + (T0[name] + 2 * t)
                        wait(ve, w_used, used + 1)
                        nc.vector.tensor_tensor(gate_r[:, :], ps[:, 2 * t, :], inv[:, :], ALU.mult).then_inc(tile_free, 1)
                        prepare(ve, unit_lo, name, i, 2 * t)
                        wait(ve, w_used, used + 2)
                        nc.vector.tensor_tensor(up_r[:, :], ps[:, 2 * t + 1, :], inv[:, :], ALU.mult).then_inc(tile_free, 1)
                        wait(ve, tile_free, tile + 2)
                        wait(ve, act_done, n + 1)
                        nc.vector.tensor_tensor(h[:, :], act[:, :], up_r[:, :], ALU.mult).then_inc(h_new, 1)
                        prepare(ve, unit_lo, name, i, 2 * t + 1)
                        wait(ve, h_hi, n + 1)
                        nc.vector.tensor_tensor(chunk(hid_lo, 2 * i + t), h[:, :],
                                                chunk(hid_hi, 2 * i + t).bitcast(F32), ALU.subtract).then_inc(h_lo, 1)

                with ve.Fori(0, FC // 2 - 1) as i:
                    body(i)
                body(FC // 2 - 1)

            ffn(0, 1)

            def down0_body(i):
                for u in range(8):
                    if u % 4 == 3:
                        t = u // 4
                        m = 2 * i + t
                        residual(m, t, i * 8 + (U0["down0"] + u + 1))
                        wait(ve, tile_free, i * 2 + (T0["down0"] + t + 1))
                        gain_lo(m, m + 2 * DC, "mix1")
                    prepare(ve, unit_lo, "down0", i, u)

            with ve.Fori(0, 3) as i:
                down0_body(i)
            down0_body(3)

            L0, B0 = U0["latent"], T0["latent"]
            make_inv(ve, 2)
            for c in range(LC):
                ve.wait_ge(w_used, L0 + c + 1)
                nc.vector.tensor_tensor(c_kv[:, c, :], ps[:, c, :], inv[:, :], ALU.mult).then_inc(tile_free, 1)
                prepare(ve, unit_lo, "latent", 0, c)
            ve.wait_ge(w_used, L0 + LC + 1)
            ve.wait_ge(tables_in, 32)
            nc.vector.tensor_tensor(k_rope[NOPE:QK, :], ps[NOPE:QK, 2, :], rope[NOPE:QK, :], ALU.mult).then_inc(rope_step, 1)
            nc.vector.tensor_tensor(rope_s[NOPE:QK, :], ps[QK:P, 2, :], rope[QK:P, :], ALU.mult).then_inc(tile_free, 1)
            ve.wait_ge(rope_step, 1)
            ve.wait_ge(tile_free, B0 + LC + 1)
            nc.vector.tensor_tensor(k_rope[NOPE:QK, :], k_rope[NOPE:QK, :], rope_s[NOPE:QK, :], ALU.add).then_inc(rope_step, 1)
            ve.wait_ge(rope_step, 2)
            nc.vector.tensor_tensor(k_rope[NOPE:QK, :], k_rope[NOPE:QK, :], inv[NOPE:QK, :], ALU.mult).then_inc(k_rope_done, 1)
            prepare(ve, unit_lo, "latent", 0, LC)

            def c_q_out(c):
                ve.wait_ge(w_used, L0 + LC + 2 + c)
                nc.vector.tensor_tensor(c_q[:, c, :], ps[:, (3, 0)[c], :], inv[:, :], ALU.mult).then_inc(tile_free, 1)

            def latent_lo(k, n_inv, g):
                make_inv(ve, n_inv, inv_lat)
                c_ = (c_kv, c_q)[k]
                for c in range(LC):
                    nc.vector.tensor_tensor(c_[:, c, :], c_[:, c, :], inv_lat[:, :], ALU.mult).then_inc(lat_scaled, 1)
                if k == 0:
                    c_q_out(0)
                for c in range(LC):
                    n = LC * k + c
                    ve.wait_ge(lat_hi, n + 1)
                    nc.vector.scalar_tensor_tensor(hid_lo[:, LAT + n, :], c_[:, c, :],
                                                   gain[:, rows[g] + c:rows[g] + c + 1],
                                                   hid_hi[:, LAT + n, :].bitcast(F32), ALU.mult,
                                                   ALU.subtract).then_inc(lat_lo, 1)

            latent_lo(0, 3, "kv_norm")
            prepare(ve, unit_lo, "latent", 0, LC + 1)
            c_q_out(1)
            prepare(ve, unit_lo, "latent", 0, LC + 2)

            def v_copy(n):
                ve.wait_ge(v_prod, n + 1)
                nc.vector.tensor_copy(v_nat[:, n % TB, (n // TB) * 512:(n // TB + 1) * 512],
                                      ps[:, 4 + n % 3, :]).then_inc(v_out, 1)

            latent_lo(1, 4, "q_norm")
            for n in range(TB):
                v_copy(n)
            for u in range(4):
                prepare(ve, unit_lo, "kv_up", 0, u)

            def rope_q(hd, par):
                wait(ve, q_prod, hd + 1)
                wait(ve, q_rope, hd)
                nc.vector.tensor_tensor(rope_s[NOPE:QK, :], ps[QK:P, 7, :], rope[QK:P, :], ALU.mult).then_inc(q_step, 1)
                nc.vector.tensor_tensor(q_T[NOPE:QK, par, :], ps[NOPE:QK, 7, :], rope[NOPE:QK, :], ALU.mult).then_inc(q_step, 1)

            rope_q(0, 0)
            for n in range(TB, 2 * TB):
                v_copy(n)
                if n == TB + 1:
                    rope_q(1, 1)
            prepare(ve, unit_lo, "q_up", 0, 0)

            def row_max(hd, par):
                wait(ve, p_turned, 3 * (hd - 2) + 3)
                for n, j in enumerate((3, 1, 2, 0)):
                    W = (j + 1) * P
                    if n < 3:
                        wait_apart(ve, s_prod, 3 * hd + (n + 1))
                    bank, col = {3: (0, 0), 1: (2, 0), 2: (1, 0), 0: (1, 384)}[j]
                    ins = nc.vector.tensor_tensor_reduce(
                        prob[:, par, L_OFF[j]:L_OFF[j] + W], ps[:, bank, col:col + W], mask[:, S - W:S],
                        1.0, -3.0e38, ALU.add, ALU.max, mx[:, par, j:j + 1])
                    if n != 2:
                        ins.then_inc(s_read, 1)
                wait(ve, s_read, 3 * hd + 3)
                nc.vector.tensor_scalar(neg_mx[:, par, :], mx[:, par, :], -SCALE, None, ALU.mult).then_inc(mx_neg, 1)

            def turned_copy(hd, par):
                wait(ve, p_turned, 3 * hd + 1)
                wait(ve, pv_done, hd - 1)
                nc.vector.tensor_copy(prob_Ts[par][:, 0, 0:512], ps[:, 3, :]).then_inc(pt_dve, 1)

            def normalise(hd, par):
                wait(ve, exp_done, hd + 1)
                wait(ve, p_ready, hd - 1)
                nc.vector.reciprocal(rec[:, par, :], sums[:, par, :]).then_inc(rec_done, 1)
                wait(ve, rec_done, hd + 1)
                for j in range(TB):
                    blk = prob[:, par, L_OFF[j]:L_OFF[j] + (j + 1) * P]
                    ins = nc.vector.tensor_scalar(blk, blk, rec[:, par, j:j + 1], None, ALU.mult)
                ins.then_inc(p_ready, 1)

            def head_out(pair):
                wait(ve, o_hi, pair + 1)
                nc.vector.tensor_tensor(chunk(hid_lo, pair), ps[:, 6, :], chunk(hid_hi, pair).bitcast(F32),
                                        ALU.subtract).then_inc(o_lo, 1)

            def attend(i, first=False, ahead=True, prep=True):
                for par in range(2):
                    row_max(2 * i + par, par)
                    if not (first and par == 0):
                        turned_copy(2 * i + (par - 1), 1 - par)
                    normalise(2 * i + par, par)
                    if ahead:
                        rope_q(2 * i + (2 + par), par)
                if not first:
                    head_out(i - 1)
                if prep:
                    unit_lo(ve, "q_up", i + 2, 0)

            attend(0, first=True)
            attend(1)
            with ve.Fori(2, PAIRS - 2) as i:
                attend(i)
            attend(PAIRS - 2, prep=False)
            for v in range(U0["mla_out"], U0["mla_out"] + 4):
                unit_lo(ve, *plan["home"][v])
            attend(PAIRS - 1, ahead=False, prep=False)
            turned_copy(HEADS - 1, 1)
            head_out(PAIRS - 1)

            out_body("mla_out", 0, "ffn1", 3)
            out_body("mla_out", 1, "ffn1", 3)
            ffn(1, 5)

            def copy_out(m, bank):
                wait(ve, out_turned, m + 1)
                nc.vector.tensor_copy(o_nat[:, :, ds(m * P, P)],
                                      ps[:, bank, :].rearrange("p (t f) -> p t f", t=TB)).then_inc(out_nat, 1)

            def down1_body(i, first=False):
                for u in range(8):
                    if u == 2 and not first:
                        copy_out(2 * i - 1, 5)
                    if u == 6:
                        copy_out(2 * i, 4)
                    if u % 4 == 3:
                        residual(2 * i + u // 4, u // 4, i * 8 + (U0["down1"] + u + 1))
                    prepare(ve, unit_lo, "down1", i, u)

            down1_body(0, first=True)
            with ve.Fori(1, 3) as i:
                down1_body(i)
            down1_body(3)
            copy_out(DC - 1, 5)
            ve.wait_ge(root_done, 7)
            nc.vector.reciprocal(inv_c, root_c).then_inc(inv_done, 1)
            ve.wait_ge(inv_done, 7)
            ve.wait_ge(out_nat, DC)
            for t in range(0, TB, 2):
                nc.vector.tensor_scalar(o_nat[:, t, :], o_nat[:, t, :], inv_c[:, t:t + 1], None, ALU.mult).then_inc(out_final[0], 1)

        @block.tensor
        def _(pe):
            pe.wait_ge(ident_in, 16)
            for m in range(DC):
                if m == 2:
                    pe.wait_ge(gain_in, 16 * 6)
                    nc.tensor.transpose(ps[:, 4, 0:G_ROWS], gain_rows[0:G_ROWS, :],
                                        ident[0:G_ROWS, 0:G_ROWS]).then_inc(gain_turned, 1)
                if m % 2 == 0:
                    pe.wait_ge(x_in[m // 2], 16)
                if m >= TILE_BANKS:
                    pe.wait_ge(tile_free, m - TILE_BANKS + 1)
                for t in range(TB):
                    ins = nc.tensor.transpose(ps[:, m % TILE_BANKS, t * P:(t + 1) * P],
                                              x_nat[:, t, m * P:(m + 1) * P], ident)
                ins.then_inc(x_turned, 1)

            def wide_phase(name, ready, ready0, stat=None):
                first_two(name, ready, ready0, stat)
                for u in range(2, shape[name][0]):
                    chunk_products(name, 0, u, every, ready, ready0)
                later_bodies(name, ready, ready0)

            def later_bodies(name, ready, ready0):
                with pe.Fori(1, shape[name][1]) as i:
                    for u in range(shape[name][0]):
                        chunk_products(name, i, u, every, ready, ready0)

            def down_tile(name, i, t, turn=None):
                l = int(name[-1])
                for q in range(4):
                    u = 4 * t + q
                    v, s, _, _ = unit_numbers(name, i, u)
                    if q == 0:
                        tile_wait(pe, name, i, t)
                    wait(pe, w_lo, v + 1)
                    c0, n = DOWN[q]
                    for k in range(n):
                        c = c0 + k
                        if t == 0 and (k == 0 or c >= FC - 2):
                            upto = c if c >= FC - 2 else min(c0 + n - 1, FC - 3)
                            pe.wait_ge(h_lo, l * FC + upto + 1)
                        col = slice(k * P, k * P + P)
                        ins = product(ps[:, t, :], wgt_hi[:, s, col], wgt_lo[:, s, col], hid_hi[:, c, :],
                                      hid_lo[:, c, :], c == 0, c == FC - 1)
                    ins.then_inc(w_used, 1)
                    if q == 1 and turn is not None:
                        turn()

            for k in every:
                chunk_products("conv_in", 0, 0, [k], x_lo, 0)
                chunk_products("conv_in", 0, 1, [k], x_lo, 0)
            chunk_products("conv_in", 0, 2, early[:4], x_lo, 0)
            statistic(sq_added, DC)
            chunk_products("conv_in", 0, 2, every[4:], x_lo, 0)
            later_bodies("conv_in", x_lo, 0)
            wide_phase("conv_out", y_lo, 0)
            wide_phase("ffn0", x_lo, DC, stat=2 * DC)
            for t in range(2):
                down_tile("down0", 0, t)
            with pe.Fori(1, 4) as i:
                for t in range(2):
                    down_tile("down0", i, t)

            first_two("latent", x_lo, 2 * DC, 3 * DC)
            chunk_products("latent", 0, 2, every, x_lo, 2 * DC)
            chunk_products("latent", 0, 3, every[:3], x_lo, 2 * DC)
            statistic(lat_sum, 1)
            chunk_products("latent", 0, 3, every[3:], x_lo, 2 * DC)
            chunk_products("latent", 0, 4, every, x_lo, 2 * DC)

            def lat(part, n):
                return part[:, LAT + n, :]

            q_slot = shape["q_up"][2][0]

            def q_product(hd, par, pair):
                wait(pe, q_nope, hd)
                wait(pe, q_rope, hd)
                if par == 0:
                    wait(pe, w_lo, pair + (U0["q_up"] + 1))
                for c in range(LC):
                    col = slice((2 * c + par) * P, (2 * c + par + 1) * P)
                    ins = product(ps[:, 7, :], wgt_hi[:, q_slot, col], wgt_lo[:, q_slot, col], lat(hid_hi, LC + c),
                                  lat(hid_lo, LC + c), c == 0, c == LC - 1)
                return ins

            def q_pair(pair, par):
                hd = 2 * pair + par
                ins = q_product(hd, par, pair)
                ins.then_inc(q_prod, 1)

            def q_used(pair):
                wait(pe, q_prod, 2 * pair + 2)
                pe.sem_inc(w_used, 1)

            n_k, n_v = 0, 0
            for half in range(2):
                units = [U0["kv_up"] + 2 * half + n for n in range(2)]
                slot = plan["slots"][units[0]]
                pe.wait_ge(w_lo, units[1] + 1)
                for pair in range(4):
                    if n_k < 4:
                        pe.wait_ge(tile_free, plan["tile0"]["mla_out"])
                    else:
                        pe.wait_ge(k_out, n_k - 3)
                    s = slot + pair // 2
                    for c in range(LC):
                        if n_k == 0:
                            pe.wait_ge(lat_lo, c + 1)
                        col = (2 * c + pair % 2) * P
                        wh, wl = (part[:, s, col:col + P] for part in (wgt_hi, wgt_lo))
                        ins = product(ps[:, n_k % 4, :], wh, wl, lat(hid_hi, c), lat(hid_lo, c), c == 0, c == LC - 1)
                    ins.then_inc(k_prod, 1)
                    n_k += 1
                if half == 0:
                    statistic(lat_sum, 2)
                else:
                    pe.wait_ge(lat_lo, 2 * LC)
                    pe.wait_ge(root_done, 5)
                    q_pair(0, 0)
                for b in range(TB):
                    if n_v >= 3:
                        pe.wait_ge(v_out, n_v - 2)
                    tok = slice(b * P, (b + 1) * P)
                    for c in range(LC):
                        vh, vl = (part[:, slot:slot + 2, 512 + c * 256:768 + c * 256] for part in (wgt_hi, wgt_lo))
                        acc = ps[:, 4 + n_v % 3, :].rearrange("p (s n) -> p s n", s=2)
                        nc.tensor.matmul(acc, lat(hid_hi, c)[:, tok], vh, start=c == 0, stop=False)
                        nc.tensor.matmul(acc, lat(hid_hi, c)[:, tok], vl, start=False, stop=False)
                        ins = nc.tensor.matmul(acc, lat(hid_lo, c)[:, tok], vh, start=False, stop=c == LC - 1)
                    ins.then_inc(v_prod, 1)
                    n_v += 1
                    if half == 1 and b == 1:
                        q_pair(0, 1)
                pe.wait_ge(v_prod, n_v)
                pe.wait_ge(k_prod, n_k)
                pe.sem_inc(w_used, 2)

            q_used(0)
            pe.wait_ge(k_out, PAIRS)
            pe.wait_ge(k_rope_set, 1)

            def logits(hd, par):
                wait(pe, q_nope, hd + 1)
                wait(pe, q_rope, hd + 1)
                for n, js in enumerate(((3,), (1,), (2, 0))):
                    wait(pe, s_read, 3 * (hd - 1) + (n + 1))
                    for j in js:
                        W = (j + 1) * P
                        bank, col = {3: (0, 0), 1: (2, 0), 2: (1, 0), 0: (1, 384)}[j]
                        ins = nc.tensor.matmul(ps[:, bank, col:col + W], q_T[0:QK, par, j * P:(j + 1) * P],
                                               k_T[0:QK, ds(hd, 1), 0:W].rearrange("p a w -> p (a w)"),
                                               start=True, stop=True)
                    ins.then_inc(s_prod, 1)

            def turn(hd, par):
                wait(pe, p_ready, hd + 1)
                for n, bs in enumerate(((0,), (2,), (1, 3))):
                    if n == 0:
                        wait(pe, pt_dve, hd)
                    if n == 1:
                        wait(pe, pt_act, hd)
                    for b in bs:
                        bank, col = {0: (3, 0), 2: (5, 0), 1: (4, 0), 3: (4, 384)}[b]
                        for j in range(b, TB):
                            ins = nc.tensor.transpose(ps[:, bank, col + (j - b) * P:col + (j - b + 1) * P],
                                                      prob[:, par, L_OFF[j] + b * P:L_OFF[j] + (b + 1) * P], ident)
                    ins.then_inc(p_turned, 1)

            def weigh(hd, par, pair):
                wait(pe, pt_dve, hd + 1)
                wait(pe, pt_act, hd + 1)
                wait(pe, v_ready, hd + 1)
                if par == 0:
                    wait(pe, o_lo, pair)
                for b in range(TB):
                    n = (TB - b) * P
                    ins = nc.tensor.matmul(ps[VD * par:VD * par + VD, 6, b * P:S], v_head[:, par, b, :],
                                           prob_Ts[par][:, 0, PT_OFF[b]:PT_OFF[b] + n], start=b == 0, stop=b == TB - 1)
                ins.then_inc(pv_done, 1)

            def attend(i, first=False, ahead=True):
                for par in range(2):
                    logits(2 * i + par, par)
                    if not (first and par == 0):
                        turn(2 * i + (par - 1), 1 - par)
                    if not first:
                        weigh(2 * i + (par - 2), par, i - 1)
                    if ahead:
                        q_pair(i + 1, par)
                if ahead:
                    q_used(i + 1)

            attend(0, first=True)
            attend(1)
            with pe.Fori(2, PAIRS - 1) as i:
                attend(i)
            attend(PAIRS - 1, ahead=False)
            pe.wait_ge(s_read, 3 * HEADS)
            chunk_products("mla_out", 0, 0, every[:6], o_lo, 0)
            turn(HEADS - 1, 1)
            weigh(HEADS - 2, 0, PAIRS - 1)
            chunk_products("mla_out", 0, 1, every[:6], o_lo, 0)
            weigh(HEADS - 1, 1, PAIRS - 1)
            chunk_products("mla_out", 0, 0, [6], o_lo, 0)
            chunk_products("mla_out", 0, 1, [6], o_lo, 0)
            chunk_products("mla_out", 0, 2, early, o_lo, 0)
            for u in range(3):
                chunk_products("mla_out", 0, u, late, o_lo, 0)
            pe.wait_ge(pt_dve, HEADS)
            chunk_products("mla_out", 0, 3, every, o_lo, 0)
            later_bodies("mla_out", o_lo, 0)
            wide_phase("ffn1", x_lo, 3 * DC, stat=4 * DC)

            def turn_out(m, buf):
                wait(pe, out_scaled, m + 1)
                wait(pe, out_nat, m)
                for t in range(TB):
                    ins = nc.tensor.transpose(ps[:, 4 + buf, t * P:(t + 1) * P], o_chunk[:, buf, t * P:(t + 1) * P], ident)
                ins.then_inc(out_turned, 1)

            down_tile("down1", 0, 0)
            down_tile("down1", 0, 1, turn=lambda: turn_out(0, 0))
            with pe.Fori(1, 4) as i:
                down_tile("down1", i, 0, turn=lambda: turn_out(2 * i - 1, 1))
                down_tile("down1", i, 1, turn=lambda: turn_out(2 * i, 0))
            turn_out(DC - 1, 1)
            pe.wait_ge(sq_added, 5 * DC)
            pe.wait_ge(root_done, 6)
            for t in range(TB):
                ins = nc.tensor.matmul(ps[:, STAT_BANK, t:t + 1], sq_sum[:, t * P:(t + 1) * P], ones[:, 0:1],
                                       start=True, stop=True)
            ins.then_inc(stat_done, 1)


_INS = ["x", "norm_mix_g", "norm_ffn_g", "ffn_w_gate", "ffn_w_up", "ffn_w_down", "final_norm_g", "conv_w_in",
        "conv_w", "conv_w_out", "mla_w_dq", "mla_q_norm_g", "mla_w_uq", "mla_w_dkv", "mla_kv_norm_g",
        "mla_w_ukv", "mla_w_o"]


def shape_constants(seq, rope_dim, theta=10000.0):
    import numpy as np

    ident = np.eye(P, dtype=np.float32)
    mask = np.zeros((P, seq), np.float32)
    mask[0:P // 2, seq - P // 2:seq] = -1e30
    inv = (np.float32(theta) ** (-np.arange(0, rope_dim, 2, dtype=np.float32) / np.float32(rope_dim))).astype(np.float32)
    ang = inv[:, None] * np.arange(seq, dtype=np.float32)[None, :]
    cos, sin = np.cos(ang), np.sin(ang)
    rope = np.zeros((P, seq), np.float32)
    rope[64:96] = np.concatenate([cos, cos])
    rope[96:128] = np.concatenate([-sin, sin])
    return np.concatenate([ident, mask, rope], axis=1).astype(np.float32)


def kernel(**inputs):
    import numpy as np
    import concourse.bacc as bacc
    from concourse.bass_utils import run_bass_kernel_spmd as run

    nc = bacc.Bacc("TRN2", target_bir_lowering=False, num_devices=1)
    arrays, args = {}, {}
    for name in _INS:
        a = np.ascontiguousarray(inputs[name])
        arrays[f"in_{name}"] = a
        args[name] = nc.dram_tensor(f"in_{name}", a.shape, mybir.dt.from_np(a.dtype), kind="ExternalInput").ap()
    shape = inputs["x"].shape
    table = shape_constants(shape[1], 32)
    arrays["constants"] = table
    consts = nc.dram_tensor("constants", table.shape, F32, kind="ExternalInput").ap()
    out = nc.dram_tensor("out", shape, F32, kind="ExternalOutput").ap()
    trunk_kernel(nc, args, consts, out)
    r = run(nc, [arrays], core_ids=[0])
    return r.results[0]["out"]
```

```python
from contextlib import ExitStack

import concourse.bass as bass
from concourse import mybir

F32 = mybir.dt.float32
F32R = mybir.dt.float32r
ACT = mybir.ActivationFunctionType
ALU = mybir.AluOpType
ds = bass.ds

P = 128
EPS = 1e-6
X_BANK, X_BANKS = 3, 4
STAT_BANK = 7


def make_plan(n_hidden):
    shape = {
        "conv_in": (3, 8, [0, 1, 2], 3, [0, 1, 2]),
        "conv_out": (4, 2, [0, 1, 2, 3], 4, [0, 1, 2, 3]),
        "ffn0": (4, n_hidden // 2, [0, 1, 2, 3], 4, [0, 1, 2, 3]),
        "down0": (8, 4, [0, 1, 2, 3] * 2, 2, [0, 1]),
        "latent": (5, 1, [0, 1, 2, 3, 0], 5, [0, 1, 2, 3, 4]),
        "kv_up": (4, 1, [2, 3, 0, 1], 0, []),
        "q_first": (1, 1, [3], 0, []),
        "q_up": (1, 7, [2], 0, []),
        "mla_out": (4, 2, [0, 1, 2, 3], 4, [0, 1, 2, 3]),
        "ffn1": (4, n_hidden // 2, [0, 1, 2, 3], 4, [0, 1, 2, 3]),
        "down1": (8, 4, [0, 1, 2, 3] * 2, 2, [0, 1]),
    }
    plan = {"shape": shape, "unit0": {}, "tile0": {}, "home": []}
    slots, prev_unit, nth = [], [], []
    last, count = {}, {}
    banks = []
    for name, (ub, n, unit_slots, tb, tile_banks) in shape.items():
        plan["unit0"][name] = len(slots)
        plan["tile0"][name] = len(banks)
        for i in range(n):
            for u in range(ub):
                s, v = unit_slots[u], len(slots)
                slots.append(s)
                prev_unit.append(last.get(s))
                count[s] = count.get(s, 0) + 1
                nth.append(count[s])
                last[s] = v
                plan["home"].append((name, i, u))
            banks += tile_banks
    prev_tile, seen = [], {}
    for t, b in enumerate(banks):
        prev_tile.append(seen.get(b))
        seen[b] = t
    after, trigger = {}, -1
    for w, p in enumerate(prev_unit):
        trigger = max(trigger, -1 if p is None else p)
        after.setdefault(trigger, []).append(w)
    plan.update(slots=slots, prev_unit=prev_unit, nth=nth, prev_tile=prev_tile, after=after,
                units=len(slots), tiles=len(banks))
    return plan


def trunk_kernel(nc, w, consts, out):
    x_dram = w["x"].rearrange("b s d -> (b s) d")
    out_dram = out.rearrange("b s d -> (b s) d")
    S, D = x_dram.shape
    F = w["ffn_w_gate"].shape[2]
    DC = D // P
    FC = F // P
    TB = S // P
    HEADS, NOPE, ROPE, VD = 16, 64, 32, 64
    QK = NOPE + ROPE
    HALF = ROPE // 2
    LORA = w["mla_w_dq"].shape[2]
    LC = LORA // P
    SCALE = float(QK) ** -0.5
    PAIRS = HEADS // 2
    PAIR_SRC = 2 * QK
    assert (S, D, DC, TB, LC) == (512, 1024, 8, 4, 2) and FC % 2 == 0

    plan = make_plan(FC)
    U0, T0, shape = plan["unit0"], plan["tile0"], plan["shape"]
    quarter = [FC // 4 + (q < FC % 4) for q in range(4)]
    DOWN = [(sum(quarter[:q]), quarter[q]) for q in range(4)]

    rows = {}
    at = 0
    for name, n in (("mix0", DC), ("mix1", DC), ("ffn0", DC), ("ffn1", DC), ("final", DC),
                    ("tap0", DC), ("tap1", DC), ("tap2", DC), ("q_norm", LC), ("kv_norm", LC)):
        rows[name] = at
        at += n
    G_ROWS = at

    L_OFF = [P * j * (j + 1) // 2 for j in range(TB)]
    L_COLS = L_OFF[-1] + TB * P
    PT_OFF = {0: 0, 1: 512, 3: 896, 2: 1024}

    with ExitStack() as ctx:
        cursor = [0]
        ARENA = 207 * 1024
        arena = ctx.enter_context(nc.sbuf_tensor("arena", [P, ARENA // 4], F32))
        base = nc.sbuf_base - ARENA

        def place(name, dims, dt, offset=None):
            size = 4
            for n in dims[1:]:
                size *= n
            size = -(-size // 32) * 32
            if offset is None:
                offset = cursor[0]
                cursor[0] += size
            assert offset + size <= ARENA
            return nc.alloc_sbuf_tensor_at(name, dims, dt, offset=base + offset), offset, offset + size

        xT, _, _ = place("xT", [P, DC, S], F32)
        xg_hi, XG, _ = place("xg_hi", [P, DC, S], F32R)
        xg_lo, _, XG_END = place("xg_lo", [P, DC, S], F32R)
        hid_hi, HID, _ = place("hid_hi", [P, FC, S], F32R)
        hid_lo, HL, HID_END = place("hid_lo", [P, FC, S], F32R)
        wgt_hi, _, _ = place("wgt_hi", [P, 4, 1024], F32R)
        wgt_lo, _, _ = place("wgt_lo", [P, 4, 1024], F32R)
        raw, _, _ = place("raw", [P, 4, 1024], F32)
        inv, _, _ = place("inv", [P, S], F32)
        sq_sum, _, _ = place("sq_sum", [P, S], F32)
        sq, SQ, _ = place("sq", [P, S], F32)
        root, _, _ = place("root", [P, S], F32, SQ)
        ident_t, _, _ = place("ident", [P, P], F32)
        ident = ident_t[:, :]
        ones, _, _ = place("ones", [P, P], F32)
        gain, _, _ = place("gain", [P, G_ROWS], F32)
        small, _, _ = place("small", [P, 64], F32)
        _, TMP, _ = place("tmp_region", [P, 5 * S + 2], F32)
        c_r, _, e = place("c_r", [P, S], F32, TMP)
        x_r, _, e = place("x_r", [P, S], F32, e)
        z, _, e = place("z", [P, S + 2], F32, e)
        cv, _, e = place("cv", [P, S], F32, e)
        y, _, e = place("y", [P, S], F32, e)
        gate_r, _, e = place("gate_r", [P, S], F32, TMP)
        up_r, _, e = place("up_r", [P, S], F32, e)
        act, _, e = place("act", [P, S], F32, e)
        h, _, e = place("h", [P, S], F32, e)
        q_T, _, e = place("q_T", [P, 2, S], F32, TMP)
        rope_s, _, e = place("rope_s", [P, S], F32, e)
        k_rope, _, e = place("k_rope", [P, S], F32, e)
        inv_lat, _, e = place("inv_lat", [P, S], F32, e)
        lat_square, _, _ = place("lat_square", [P, LC, S], F32, TMP)
        x_nat, _, _ = place("x_nat", [P, TB, D], F32, HID)
        gain_rows, _, _ = place("gain_rows", [P, P], F32, HL)
        LAT = DC
        FREE_HI, FREE_LO = HID + (LAT + 2 * LC) * S * 4, HL + (LAT + 2 * LC) * S * 4
        k_T, _, e = place("k_T", [QK, HEADS, S], F32, XG)
        assert e <= XG_END
        v_nat, _, e = place("v_nat", [P, TB, HEADS * VD], F32, FREE_HI)
        v_head, _, e = place("v_head", [P, 2, TB, VD], F32, e)
        mask, _, e = place("mask", [P, S], F32, e)
        assert e <= HL
        prob, _, e = place("prob", [P, 2, L_COLS], F32, FREE_LO)
        lat_ms, _, _ = place("lat_ms", [P, S], F32, FREE_LO)
        c_kv, _, e2 = place("c_kv", [P, LC, S], F32, e)
        c_q, _, e2 = place("c_q", [P, LC, S], F32, e2)
        rope, _, e2 = place("rope", [P, S], F32, e2)
        assert e2 <= HID_END
        prob_T, _, e = place("prob_T", [P, 1, L_COLS], F32, e)
        prob_T2, _, e3 = place("prob_T2", [P, 1, L_COLS], F32, cursor[0])
        cursor[0] = e3
        prob_Ts = [prob_T, prob_T2]
        assert e <= HID_END
        o_nat, _, e = place("o_nat", [P, TB, D], F32, XG)
        o_chunk, _, e = place("o_chunk", [P, 2, S], F32, TMP)

        mx, neg_mx, sums, rec = (small[:, 8 * n:8 * n + 8].rearrange("p (b j) -> p b j", b=2) for n in range(4))
        root_c, inv_c = small[:, 32:32 + TB], small[:, 40:40 + TB]

        ps = ctx.enter_context(nc.psum_tensor("ps", [P, 8, 512], F32))

        def sem(name):
            return ctx.enter_context(nc.semaphore(name))

        ident_in, tables_in, mix_in, gain_in = sem("ident_in"), sem("tables_in"), sem("mix_in"), sem("gain_in")
        x_in = [sem(f"x_in{c}") for c in range(4)]
        raw_in = [sem(f"raw_in{s}") for s in range(4)]
        w_hi, w_lo, w_used = sem("w_hi"), sem("w_lo"), sem("w_used")
        ones_set, z_pad, gain_turned, gain_ready = sem("ones_set"), sem("z_pad"), sem("gain_turned"), sem("gain_ready")
        x_turned, x_copied, sq_other, sq_rest = sem("x_turned"), sem("x_copied"), sem("sq_other"), sem("sq_rest")
        tile_free = sem("tile_free")
        x_hi, x_lo = sem("x_hi"), sem("x_lo")
        sq_zero, sq_new, sq_added = sem("sq_zero"), sem("sq_new"), sem("sq_added")
        stat_done, root_done, inv_done = sem("stat_done"), sem("root_done"), sem("inv_done")
        conv_step, y_new, y_hi, y_lo = sem("conv_step"), sem("y_new"), sem("y_hi"), sem("y_lo")
        half_done, x_last, sq_last = sem("half_done"), sem("x_last"), sem("sq_last")
        act_done, h_new, h_hi, h_lo = sem("act_done"), sem("h_new"), sem("h_hi"), sem("h_lo")
        rope_step, k_rope_done = sem("rope_step"), sem("k_rope_done")
        lat_sq, ms_done, inv_both, lat_scaled = sem("lat_sq"), sem("ms_done"), sem("inv_both"), sem("lat_scaled")
        lat_hi, lat_lo = sem("lat_hi"), sem("lat_lo")
        k_prod, k_out, v_prod, v_out = sem("k_prod"), sem("k_out"), sem("v_prod"), sem("v_out")
        k_rope_early, k_rope_late = sem("k_rope_early"), sem("k_rope_late")
        q_prod, q_out, q_sine, q_cosine, q_rope = (sem(n) for n in ("q_prod", "q_out", "q_sine", "q_cosine", "q_rope"))
        s_prod, s_read, mx_neg, exp_done = sem("s_prod"), sem("s_read"), sem("mx_neg"), sem("exp_done")
        rec_done, p_ready, p_turned = sem("rec_done"), sem("p_ready"), sem("p_turned")
        pt_ready, v_ready, pv_done = sem("pt_ready"), sem("v_ready"), sem("pv_done")
        o_hi, o_lo = sem("o_hi"), sem("o_lo")
        out_scaled, out_turned, out_nat, stored = (sem(n) for n in ("out_scaled", "out_turned", "out_nat", "stored"))
        out_final = [sem("out_final_even"), sem("out_final_odd")]

        passed = {e.engine: sem(f"passed_{n}") for n, e in (("sp", nc.sync), ("pool", nc.gpsimd), ("dve", nc.vector))}

        def wait(eng, semaphore, value):
            if isinstance(value, int) and value <= 0:
                return
            eng.wait_ge(semaphore, value)

        def wait_apart(eng, semaphore, value):
            wait(eng, semaphore, value)
            if not isinstance(value, int):
                eng.sem_inc(passed[eng.engine], 1)

        def chunked(m):
            return m.rearrange("(c p) n -> p c n", p=P)

        conv_in, conv_out = chunked(w["conv_w_in"][0]), chunked(w["conv_w_out"][0])
        w_dq, w_uq = chunked(w["mla_w_dq"][0]), chunked(w["mla_w_uq"][0])
        w_dkv, w_ukv, w_o = chunked(w["mla_w_dkv"][0]), chunked(w["mla_w_ukv"][0]), chunked(w["mla_w_o"][0])
        gates = [chunked(w["ffn_w_gate"][l]) for l in range(2)]
        ups = [chunked(w["ffn_w_up"][l]) for l in range(2)]
        downs = [chunked(w["ffn_w_down"][l]) for l in range(2)]

        def source(name, i, u):
            if name == "conv_in":
                return conv_in[:, :, ds(i * P + (1, 2, 0)[u] * D, P)], DC, P
            if name in ("conv_out", "mla_out"):
                m = conv_out if name == "conv_out" else w_o
                return m[:, :, ds(i * (4 * P) + u * P, P)], DC, P
            if name.startswith("ffn"):
                m = (gates, ups)[u % 2][int(name[-1])]
                return m[:, :, ds(i * (2 * P) + (u // 2) * P, P)], DC, P
            if name.startswith("down"):
                c0, n = DOWN[u % 4]
                return downs[int(name[-1])][:, c0:c0 + n, ds(i * (2 * P) + (u // 4) * P, P)], n, P
            if name == "latent":
                m, c0, n = ((w_dkv, 0, P), (w_dkv, P, P), (w_dkv, LORA + ROPE - QK, QK), (w_dq, 0, P), (w_dq, P, P))[u]
                return m[:, :, c0:c0 + n], DC, n
            if name == "kv_up":
                return w_ukv[:, :, u * 512:(u + 1) * 512], LC, 512
            pair = 0 if name == "q_first" else i + 1
            return w_uq[:, :, ds(pair * PAIR_SRC, PAIR_SRC)], LC, PAIR_SRC

        def unit_numbers(name, i, u):
            ub, n, slots, _, _ = shape[name]
            if isinstance(i, int):
                v = U0[name] + ub * i + u
                return v, plan["slots"][v], plan["prev_unit"][v], plan["nth"][v]
            used = len(set(slots))
            v1 = U0[name] + ub + u
            per_body = ub // used
            return (i * ub + (U0[name] + u), slots[u], i * ub + (plan["prev_unit"][v1] - ub),
                    i * per_body + (plan["nth"][v1] - per_body))

        def load_unit(eng, name, i, u):
            v, s, prev, _ = unit_numbers(name, i, u)
            src, n, width = source(name, i, u)
            if prev is not None:
                wait_apart(eng, w_lo, prev + 1)
            dst = raw[:, s, 0:n * width].rearrange("p (c n) -> p c n", c=n)
            eng.dma_start(dst, src).then_inc(raw_in[s], 16)

        def split_parts(name, s, n, width, part):
            dst, src = part[:, s, :], raw[:, s, 0:n * width]
            if name.startswith("q_") or width == QK:
                heads = width // QK
                d = dst[:, 0:n * heads * P].rearrange("p (c m) -> p c m", m=P)
                r = src.rearrange("p (c m) -> p c m", m=QK)
                return [(d[:, :, 0:QK], r), (d[:, :, QK:QK + HALF], r[:, :, NOPE + HALF:QK]),
                        (d[:, :, QK + HALF:P], r[:, :, NOPE:NOPE + HALF])]
            if name == "kv_up":
                r = src.rearrange("p (g m) -> p g m", m=2 * NOPE)
                return [(dst[:, o * 512:(o + 1) * 512].rearrange("p (g m) -> p g m", m=NOPE),
                         r[:, :, o * NOPE:(o + 1) * NOPE]) for o in range(2)]
            return [(dst[:, 0:n * width], src)]

        def unit_hi(eng, name, i, u):
            v, s, prev, nth = unit_numbers(name, i, u)
            _, n, width = source(name, i, u)
            eng.wait_ge(raw_in[s], nth * 16)
            if prev is not None:
                wait(eng, w_used, prev + 1)
            for dst, src in split_parts(name, s, n, width, wgt_hi):
                ins = nc.scalar.activation(dst, src, ACT.Copy)
            ins.then_inc(w_hi, 1)

        def unit_lo(eng, name, i, u):
            v, s, prev, nth = unit_numbers(name, i, u)
            _, n, width = source(name, i, u)
            wait(eng, w_hi, v + 1)
            for (dst, src), (hi, _) in zip(split_parts(name, s, n, width, wgt_lo),
                                           split_parts(name, s, n, width, wgt_hi)):
                ins = nc.vector.tensor_tensor(dst, src, hi.bitcast(F32), ALU.subtract)
            ins.then_inc(w_lo, 1)

        def prepare(eng, make, name, i, u):
            ub, n, slots, _, _ = shape[name]
            if isinstance(i, int):
                for v in plan["after"].get(U0[name] + ub * i + u, []):
                    make(eng, *plan["home"][v])
                return
            ahead = u + len(set(slots))
            make(eng, name, i + ahead // ub, ahead % ub)

        def product(acc, wh, wl, xh, xl, first, last):
            nc.tensor.matmul(acc, wh, xh, start=first, stop=False)
            nc.tensor.matmul(acc, wh, xl, start=False, stop=False)
            return nc.tensor.matmul(acc, wl, xh, start=False, stop=last)

        def tile_wait(eng, name, i, t):
            _, _, _, tb, banks = shape[name]
            if isinstance(i, int):
                prev = plan["prev_tile"][T0[name] + tb * i + t]
                if prev is not None:
                    eng.wait_ge(tile_free, prev + 1)
            else:
                wait(eng, tile_free, i * tb + (plan["prev_tile"][T0[name] + tb + t] - tb + 1))

        def chunk_products(name, i, u, ks, ready, ready0):
            pe = nc.tensor
            v, s, _, _ = unit_numbers(name, i, u)
            if ks[0] == 0:
                tile_wait(pe, name, i, u)
                wait(pe, w_lo, v + 1)
            hi, lo = (xg_hi, xg_lo) if ready is x_lo else (hid_hi, hid_lo)
            acc = ps[:, shape[name][4][u], :]
            for k in ks:
                if isinstance(i, int) and i == 0 and u == 0:
                    pe.wait_ge(ready, ready0 + k + 1)
                col = slice(k * P, k * P + P)
                ins = product(acc, wgt_hi[:, s, col], wgt_lo[:, s, col], hi[:, k, :], lo[:, k, :],
                              k == 0, k == DC - 1)
            if ks[-1] == DC - 1:
                ins.then_inc(w_used, 1)

        early, late, every = list(range(DC - 1)), [DC - 1], list(range(DC))

        def first_two(name, ready, ready0, norm=None):
            chunk_products(name, 0, 0, early, ready, ready0)
            chunk_products(name, 0, 1, early[:2], ready, ready0)
            if norm is not None:
                statistic(norm)
            chunk_products(name, 0, 1, early[2:], ready, ready0)
            chunk_products(name, 0, 0, late, ready, ready0)
            chunk_products(name, 0, 1, late, ready, ready0)

        X_POOL = DC - 3

        def squares_before(n):
            return X_POOL + (n - 1) * DC if n else 0

        ROOT = {0: 0, 1: 1, 2: 2, 3: 5, 4: 6}

        def statistic(norm):
            pe = nc.tensor
            pe.wait_ge(sq_added, squares_before(norm + 1))
            pe.wait_ge(root_done, ROOT[norm])
            nc.tensor.matmul(ps[:, STAT_BANK, :], ones[:, :], sq_sum[:, :],
                             start=True, stop=True).then_inc(stat_done, 1)

        def make_root(eng, n, width):
            eng.wait_ge(stat_done, n + 1)
            if n:
                eng.wait_ge(inv_done, n)
            nc.scalar.activation(root[:, :], ps[:, STAT_BANK, :], ACT.Sqrt, scale=1.0 / width,
                                 bias=small[:, 48:49]).then_inc(root_done, 1)

        def make_inv(eng, n, to=inv):
            eng.wait_ge(root_done, n + 1)
            nc.vector.reciprocal(to[:, :], root[:, :]).then_inc(inv_done, 1)
            eng.wait_ge(inv_done, n + 1)

        def k_rope_part(copy, n):
            return copy(k_T[NOPE:QK, 4 * n:4 * n + 4, :], k_rope[NOPE:QK, :].unsqueeze(1).broadcast_to([ROPE, 4, S]))

        block = ctx.enter_context(nc.Block())

        @block.sync
        def _(sp):
            def load_x(c):
                n = D // 4
                sp.dma_start(x_nat[:, :, c * n:(c + 1) * n],
                             x_dram.rearrange("(t p) d -> p t d", p=P)[:, :, c * n:(c + 1) * n]).then_inc(x_in[c], 16)

            sp.dma_start(ident, consts[:, 0:P]).then_inc(ident_in, 16)
            load_x(0)
            load_unit(sp, "conv_in", 0, 0)
            load_x(1)
            load_unit(sp, "conv_in", 0, 1)
            load_x(2)
            load_x(3)
            for name in shape:
                ub, n = shape[name][0:2]
                for u in range(2 if name == "conv_in" else 0, ub):
                    load_unit(sp, name, 0, u)
                if n > 1:
                    with sp.Fori(1, n) as i:
                        for u in range(ub):
                            load_unit(sp, name, i, u)
            for t in range(TB):
                sp.wait_ge(out_final[t % 2], t // 2 + 1)
                sp.dma_start(out_dram[t * P:(t + 1) * P, :], o_nat[:, t, :]).then_inc(stored, 16)
            sp.wait_ge(stored, 16 * TB)

        def latents(pool):
            pool.wait_ge(w_used, U0["latent"])
            pool.dma_start(mask[:, :], consts[:, P:P + S]).then_inc(tables_in, 16)
            pool.dma_start(rope[:, :], consts[:, P + S:P + 2 * S]).then_inc(tables_in, 16)
            def v_slice(hd, par):
                wait(pool, pv_done, hd - 1)
                nc.gpsimd.tensor_copy(v_head[:, par, :, :], v_nat[:, :, ds(hd * VD, VD)]).then_inc(v_ready, 1)

            def add_rope(hd, par):
                wait(pool, q_out, hd + 1)
                nc.gpsimd.tensor_tensor(q_T[NOPE:QK, par, :], q_T[NOPE:QK, par, :], rope[NOPE:QK, :],
                                        ALU.mult).then_inc(q_cosine, 1)
                wait(pool, q_cosine, hd + 1)
                wait(pool, q_sine, hd + 1)
                nc.gpsimd.tensor_tensor(q_T[NOPE:QK, par, :], q_T[NOPE:QK, par, :], rope_s[NOPE:QK, :],
                                        ALU.add).then_inc(q_rope, 1)

            add_rope(0, 0)
            pool.wait_ge(q_rope, 1)
            add_rope(1, 1)
            pool.wait_ge(v_out, 2 * TB)

            def heads(i, first=False, ahead=True):
                for par in range(2):
                    hd = 2 * i + par
                    if (par == 0 or ahead) and not (first and par == 0):
                        wait(pool, v_ready, hd)
                        add_rope(hd + 1, 1 - par)
                    wait(pool, q_rope, hd + (2 if par == 0 or ahead else 1))
                    v_slice(hd, par)

            heads(0, first=True)
            with pool.Fori(1, PAIRS - 1) as i:
                heads(i)
            heads(PAIRS - 1, ahead=False)

        @block.gpsimd
        def _(pool):
            nc.gpsimd.memset(ones[:, :], 1.0).then_inc(ones_set, 1)
            nc.gpsimd.memset(small[:, :], EPS).then_inc(ones_set, 1)
            nc.gpsimd.memset(z[:, 0:2], 0.0).then_inc(z_pad, 1)

            def load_gains(row, g):
                n = g.shape[0]
                pool.dma_start(gain_rows[row:row + n, :], g).then_inc(gain_in, 16)

            load_gains(rows["ffn0"], w["norm_ffn_g"].rearrange("l (r c) -> (l r) c", c=P))
            load_gains(rows["final"], w["final_norm_g"].rearrange("(r c) -> r c", c=P))
            load_gains(rows["tap0"], w["conv_w"].rearrange("a t (r c) -> (a t r) c", c=P))
            load_gains(rows["q_norm"], w["mla_q_norm_g"].rearrange("a (r c) -> (a r) c", c=P))
            load_gains(rows["kv_norm"], w["mla_kv_norm_g"].rearrange("a (r c) -> (a r) c", c=P))

            def clear_sum(n):
                if n:
                    pool.wait_ge(stat_done, ROOT[n])
                nc.gpsimd.memset(sq_sum[:, :], 0.0).then_inc(sq_zero, 1)

            def add_square(n, m, ready, count):
                wait(pool, ready, count)
                wait(pool, sq_added, m + squares_before(n))
                nc.gpsimd.tensor_tensor(sq[:, :], xT[:, ds(m, 1), :].rearrange("p a s -> p (a s)"),
                                        xT[:, ds(m, 1), :].rearrange("p a s -> p (a s)"), ALU.mult).then_inc(sq_new, 1)
                wait(pool, sq_new, m + (squares_before(n) + 1))
                pool.wait_ge(sq_zero, n + 1)
                nc.gpsimd.tensor_tensor(sq_sum[:, :], sq_sum[:, :], sq[:, :], ALU.add).then_inc(sq_added, 1)

            clear_sum(0)
            for m in range(X_POOL):
                add_square(0, m, x_copied, m + 1)
            for n, name in ((1, "conv_out"), (2, "down0"), (3, "mla_out"), (4, "down1")):
                clear_sum(n)
                with pool.Fori(0, DC - (n == 4)) as m:
                    add_square(n, m, tile_free, m + (T0[name] + 1))
                if n == 2:
                    latents(pool)

        @block.scalar
        def _(sc):
            sc.dma_start(gain_rows[0:2 * DC, :],
                         w["norm_mix_g"].rearrange("l (r c) -> (l r) c", c=P)).then_inc(mix_in, 16)

            def chunk(t, m):
                return t[:, ds(m, 1), :].rearrange("p a s -> p (a s)")

            def gain_hi(m, tile, g):
                wait(sc, tile_free, tile + 1)
                nc.scalar.activation(chunk(xg_hi, m), chunk(xT, m), ACT.Copy,
                                     scale=gain[:, ds(m + rows[g], 1)]).then_inc(x_hi, 1)

            sc.wait_ge(ones_set, 2)
            nc.scalar.activation(small[:, 56:57], small[:, 48:49], ACT.Copy)

            sc.wait_ge(gain_ready, 1)
            for m in range(DC + 1):
                if m < DC:
                    sc.wait_ge(x_turned, m + 1)
                    nc.scalar.activation(xg_hi[:, m, :], ps[:, X_BANK + m % X_BANKS, :], ACT.Copy,
                                         scale=gain[:, rows["mix0"] + m:rows["mix0"] + m + 1]).then_inc(x_hi, 1)
                if m:
                    sc.wait_ge(x_lo, m)
                    nc.scalar.activation(xT[:, m - 1, :], ps[:, X_BANK + (m - 1) % X_BANKS, :],
                                         ACT.Copy).then_inc(x_copied, 1)
                if m in (0, 3, 6):
                    unit_hi(sc, *plan["home"][m // 3])
            sc.wait_ge(x_copied, DC)
            for m, to in zip(range(X_POOL, DC), (c_r, x_r, y)):
                nc.scalar.activation(to[:, :], xT[:, m, :], ACT.Square).then_inc(sq_other, 1)
            prepare(sc, unit_hi, "conv_in", 0, 0)
            make_root(sc, 0, D)
            prepare(sc, unit_hi, "conv_in", 0, 1)

            def conv_body(i, first=False):
                if not first:
                    prepare(sc, unit_hi, "conv_in", i, 0)
                    prepare(sc, unit_hi, "conv_in", i, 1)
                wait(sc, y_new, i + 1)
                nc.scalar.activation(chunk(hid_hi, i), y[:, :], ACT.Copy).then_inc(y_hi, 1)
                prepare(sc, unit_hi, "conv_in", i, 2)

            conv_body(0, first=True)
            with sc.Fori(1, DC - 1) as i:
                conv_body(i)
            conv_body(DC - 1)

            def out_body(name, i, g):
                for u in range(4):
                    gain_hi(4 * i + u, i * 4 + (T0[name] + u), g)
                    prepare(sc, unit_hi, name, i, u)

            out_body("conv_out", 0, "ffn0")
            out_body("conv_out", 1, "ffn0")

            def ffn(l, n_root):
                name = f"ffn{l}"
                make_root(sc, n_root, D)

                def body(i):
                    for t in range(2):
                        n = 2 * i + (t + l * FC)
                        wait(sc, tile_free, i * 4 + (T0[name] + 2 * t + 1))
                        nc.scalar.activation(act[:, :], gate_r[:, :], ACT.Silu).then_inc(act_done, 1)
                        prepare(sc, unit_hi, name, i, 2 * t)
                        prepare(sc, unit_hi, name, i, 2 * t + 1)
                        wait(sc, h_new, n + 1)
                        nc.scalar.activation(chunk(hid_hi, 2 * i + t), h[:, :], ACT.Copy).then_inc(h_hi, 1)

                with sc.Fori(0, FC // 2 - 1) as i:
                    body(i)
                body(FC // 2 - 1)

            ffn(0, 1)

            def down0_body(i):
                for u in range(8):
                    if u % 4 == 3:
                        m = u // 4
                        gain_hi(2 * i + m, i * 2 + (T0["down0"] + m), "mix1")
                    prepare(sc, unit_hi, "down0", i, u)

            with sc.Fori(0, 3) as i:
                down0_body(i)
            down0_body(3)

            def square(k, c):
                sc.wait_ge(w_used, U0["latent"] + (LC + 1) * k + c + 1)
                if k:
                    sc.wait_ge(stat_done, 4)
                nc.scalar.activation(lat_square[:, c, :], ps[:, (LC + 1) * k + c, :], ACT.Square).then_inc(lat_sq, 1)

            def latent_root(k):
                n = 3 + k
                sc.wait_ge(ms_done, 2 * k + 2)
                sc.wait_ge(inv_done, n)
                nc.scalar.activation(root[:, :], lat_ms[:, :], ACT.Sqrt, scale=1.0 / LORA,
                                     bias=small[:, 48:49]).then_inc(root_done, 1)

            def latent_hi(k, g):
                for c in range(LC):
                    n = LC * k + c
                    sc.wait_ge(lat_scaled, n + 1)
                    src = (c_kv, c_q)[k][:, c, :]
                    nc.scalar.activation(hid_hi[:, LAT + n, :], src, ACT.Copy,
                                         scale=gain[:, rows[g] + c:rows[g] + c + 1]).then_inc(lat_hi, 1)

            make_root(sc, 2, D)
            for c in range(LC):
                square(0, c)
                prepare(sc, unit_hi, "latent", 0, c)
            latent_root(0)
            prepare(sc, unit_hi, "latent", 0, 2)
            latent_hi(0, "kv_norm")
            square(1, 0)
            prepare(sc, unit_hi, "latent", 0, 3)
            square(1, 1)
            prepare(sc, unit_hi, "latent", 0, 4)

            def k_copy(n):
                sc.wait_ge(k_prod, n + 1)
                for par in range(2):
                    ins = nc.scalar.activation(k_T[0:NOPE, 2 * n + par, :], ps[64 * par:64 * par + NOPE, n % 4, :], ACT.Copy)
                ins.then_inc(k_out, 1)

            for n in range(4):
                k_copy(n)
                if n == 0:
                    sc.wait_ge(k_rope_done, 1)
                    k_rope_part(nc.scalar.copy, 0).then_inc(k_rope_early, 1)
                    latent_root(1)
            latent_hi(1, "q_norm")
            k_rope_part(nc.scalar.copy, 1).then_inc(k_rope_early, 1)
            for u in range(4):
                prepare(sc, unit_hi, "kv_up", 0, u)
            for n in range(4, PAIRS):
                k_copy(n)

            def exponentials(hd, par):
                for n, js in enumerate(((3, 1), (2, 0))):
                    wait(sc, mx_neg, 2 * hd + (n + 1))
                    for j in js:
                        blk = prob[:, par, L_OFF[j]:L_OFF[j] + (j + 1) * P]
                        ins = nc.scalar.activation(blk, blk, ACT.Exp, bias=neg_mx[:, par, j:j + 1], scale=SCALE,
                                                   accum_out=sums[:, par, j:j + 1])
                    ins.then_inc(exp_done, 1)

            def turned_copy(hd, par):
                wait(sc, p_turned, 3 * hd + 1)
                wait(sc, pv_done, hd - 1)
                nc.scalar.activation(prob_Ts[par][:, 0, 0:512], ps[:, 3, :], ACT.Copy)
                wait(sc, p_turned, 3 * hd + 2)
                nc.scalar.activation(prob_Ts[par][:, 0, 1024:1280], ps[:, 5, 0:256], ACT.Copy)
                wait(sc, p_turned, 3 * hd + 3)
                nc.scalar.activation(prob_Ts[par][:, 0, 512:1024], ps[:, 4, :], ACT.Copy).then_inc(pt_ready, 1)

            def head_out(pair):
                wait(sc, pv_done, 2 * pair + 2)
                nc.scalar.activation(chunk(hid_hi, pair), ps[:, 6, :], ACT.Copy).then_inc(o_hi, 1)

            def q_copy(hd, par):
                wait(sc, q_prod, hd + 1)
                nc.scalar.activation(q_T[:, par, :], ps[:, 7, :], ACT.Copy).then_inc(q_out, 1)

            q_copy(0, 0)

            def attend(i, first=False, ahead=True):
                for par in range(2):
                    if par == 1 and ahead:
                        q_copy(2 * i + 2, 0)
                    if not first:
                        turned_copy(2 * i + (par - 2), par)
                    if par == 0:
                        q_copy(2 * i + 1, 1)
                    if par == 0 and not first:
                        unit_hi(sc, *(("q_up", i, 0) if ahead else ("mla_out", 0, 1)))
                    if par == 1 and not first:
                        head_out(i - 1)
                    exponentials(2 * i + par, par)
                    if isinstance(i, int) and par == 0 and i >= PAIRS - 2:
                        unit_hi(sc, "mla_out", 0, 2 * (i - PAIRS + 2))

            attend(0, first=True)
            attend(1)
            with sc.Fori(2, PAIRS - 2) as i:
                attend(i)
            attend(PAIRS - 2)
            attend(PAIRS - 1, ahead=False)
            turned_copy(HEADS - 2, 0)
            unit_hi(sc, "mla_out", 0, 3)
            turned_copy(HEADS - 1, 1)
            head_out(PAIRS - 1)

            out_body("mla_out", 0, "ffn1")
            out_body("mla_out", 1, "ffn1")
            ffn(1, 5)

            def down1_body(i, last=False):
                for u in range(8):
                    if u % 4 == 3 and not (last and u == 7):
                        m = 2 * i + u // 4
                        wait(sc, tile_free, i * 2 + (T0["down1"] + u // 4 + 1))
                        wait(sc, out_turned, m - 1)
                        nc.scalar.activation(o_chunk[:, u // 4, :], chunk(xT, m), ACT.Copy,
                                             scale=gain[:, ds(m + rows["final"], 1)]).then_inc(out_scaled, 1)
                    prepare(sc, unit_hi, "down1", i, u)

            down1_body(0)
            with sc.Fori(1, 3) as i:
                down1_body(i)
            down1_body(3, last=True)
            for half in range(2):
                tok = slice(half * S // 2, (half + 1) * S // 2)
                sc.wait_ge(x_last, half + 1)
                sc.wait_ge(out_turned, DC - 2)
                nc.scalar.activation(o_chunk[:, 1, tok], xT[:, DC - 1, tok], ACT.Copy,
                                     scale=gain[:, rows["final"] + DC - 1:rows["final"] + DC]).then_inc(out_scaled, 1)
                two = slice(2 * half, 2 * half + 2)
                sc.wait_ge(stat_done, 7 + half)
                nc.scalar.activation(root_c[:, two], ps[:, STAT_BANK, two], ACT.Sqrt, scale=1.0 / D,
                                     bias=small[:, 48:49]).then_inc(root_done, 1)
                sc.wait_ge(inv_done, 7 + half)
                sc.wait_ge(out_nat, DC + half)
                t = 2 * half + 1
                nc.scalar.activation(o_nat[:, t, :], o_nat[:, t, :], ACT.Copy, scale=inv_c[:, t:t + 1]).then_inc(out_final[1], 1)

        @block.vector
        def _(ve):
            def chunk(t, m):
                return t[:, ds(m, 1), :].rearrange("p a s -> p (a s)")

            ve.wait_ge(gain_turned, 1)
            nc.vector.tensor_copy(gain[:, 0:2 * DC], ps[:, STAT_BANK, 0:2 * DC]).then_inc(gain_ready, 1)
            ve.wait_ge(gain_ready, 1)

            def gain_lo(m, count, g):
                wait(ve, x_hi, count + 1)
                nc.vector.scalar_tensor_tensor(chunk(xg_lo, m), chunk(xT, m), gain[:, ds(m + rows[g], 1)],
                                               chunk(xg_hi, m).bitcast(F32), ALU.mult, ALU.subtract).then_inc(x_lo, 1)

            for m in range(DC):
                ve.wait_ge(x_hi, m + 1)
                nc.vector.scalar_tensor_tensor(xg_lo[:, m, :], ps[:, X_BANK + m % X_BANKS, :],
                                               gain[:, rows["mix0"] + m:rows["mix0"] + m + 1],
                                               xg_hi[:, m, :].bitcast(F32), ALU.mult, ALU.subtract).then_inc(x_lo, 1)
                if m in (0, 3, 6):
                    unit_lo(ve, *plan["home"][m // 3])
            for n, part in enumerate((x_r, y)):
                ve.wait_ge(sq_other, n + 2)
                if n:
                    ve.wait_ge(sq_rest, n)
                nc.vector.tensor_tensor(c_r[:, :], c_r[:, :], part[:, :], ALU.add).then_inc(sq_rest, 1)
            ve.wait_ge(gain_turned, 2)
            nc.vector.tensor_copy(gain[:, 2 * DC:G_ROWS], ps[:, STAT_BANK, 2 * DC:G_ROWS]).then_inc(gain_ready, 1)
            prepare(ve, unit_lo, "conv_in", 0, 0)
            make_inv(ve, 0)
            ve.wait_ge(z_pad, 1)
            ve.wait_ge(gain_ready, 2)

            def conv_body(i, first=False):
                unit = i * 3 + U0["conv_in"]
                step = 4 * i
                wait(ve, w_used, unit + 1)
                nc.vector.tensor_tensor(c_r[:, :], ps[:, 0, :], inv[:, :], ALU.mult).then_inc(tile_free, 1)
                prepare(ve, unit_lo, "conv_in", i, int(first))
                wait(ve, w_used, unit + 2)
                nc.vector.tensor_tensor(x_r[:, :], ps[:, 1, :], inv[:, :], ALU.mult).then_inc(tile_free, 1)
                wait(ve, tile_free, i * 3 + (T0["conv_in"] + 2))
                nc.vector.tensor_tensor(z[:, 2:S + 2], c_r[:, :], x_r[:, :], ALU.mult).then_inc(conv_step, 1)
                wait(ve, conv_step, step + 1)
                nc.vector.tensor_scalar(cv[:, :], z[:, 2:S + 2], gain[:, ds(i + rows["tap2"], 1)], None,
                                        ALU.mult).then_inc(conv_step, 1)
                wait(ve, conv_step, step + 2)
                nc.vector.scalar_tensor_tensor(x_r[:, :], z[:, 1:S + 1], gain[:, ds(i + rows["tap1"], 1)], cv[:, :],
                                               ALU.mult, ALU.add).then_inc(conv_step, 1)
                wait(ve, conv_step, step + 3)
                nc.vector.scalar_tensor_tensor(cv[:, :], z[:, 0:S], gain[:, ds(i + rows["tap0"], 1)], x_r[:, :],
                                               ALU.mult, ALU.add).then_inc(conv_step, 1)
                if not first:
                    prepare(ve, unit_lo, "conv_in", i, 1)
                wait(ve, w_used, unit + 3)
                nc.vector.tensor_tensor(c_r[:, :], ps[:, 2, :], inv[:, :], ALU.mult).then_inc(tile_free, 1)
                wait(ve, tile_free, i * 3 + (T0["conv_in"] + 3))
                wait(ve, conv_step, step + 4)
                nc.vector.tensor_tensor(y[:, :], c_r[:, :], cv[:, :], ALU.mult).then_inc(y_new, 1)
                wait(ve, y_hi, i + 1)
                nc.vector.tensor_tensor(chunk(hid_lo, i), y[:, :], chunk(hid_hi, i).bitcast(F32),
                                        ALU.subtract).then_inc(y_lo, 1)
                prepare(ve, unit_lo, "conv_in", i, 2)

            conv_body(0, first=True)
            with ve.Fori(1, DC - 1) as i:
                conv_body(i)
            conv_body(DC - 1)

            def residual(m, bank, used):
                wait(ve, w_used, used)
                nc.vector.tensor_tensor(chunk(xT, m), ps[:, bank, :], chunk(xT, m), ALU.add).then_inc(tile_free, 1)

            def out_body(name, i, g, norm):
                for u in range(4):
                    m = 4 * i + u
                    residual(m, u, i * 4 + (U0[name] + u + 1))
                    wait(ve, tile_free, i * 4 + (T0[name] + u + 1))
                    gain_lo(m, m + norm * DC, g)
                    prepare(ve, unit_lo, name, i, u)

            out_body("conv_out", 0, "ffn0", 1)
            out_body("conv_out", 1, "ffn0", 1)

            def ffn(l, n_inv):
                name = f"ffn{l}"
                make_inv(ve, n_inv)

                def body(i):
                    for t in range(2):
                        n = 2 * i + (t + l * FC)
                        used, tile = i * 4 + (U0[name] + 2 * t), i * 4 + (T0[name] + 2 * t)
                        wait(ve, w_used, used + 1)
                        nc.vector.tensor_tensor(gate_r[:, :], ps[:, 2 * t, :], inv[:, :], ALU.mult).then_inc(tile_free, 1)
                        prepare(ve, unit_lo, name, i, 2 * t)
                        wait(ve, w_used, used + 2)
                        nc.vector.tensor_tensor(up_r[:, :], ps[:, 2 * t + 1, :], inv[:, :], ALU.mult).then_inc(tile_free, 1)
                        wait(ve, tile_free, tile + 2)
                        wait(ve, act_done, n + 1)
                        nc.vector.tensor_tensor(h[:, :], act[:, :], up_r[:, :], ALU.mult).then_inc(h_new, 1)
                        prepare(ve, unit_lo, name, i, 2 * t + 1)
                        wait(ve, h_hi, n + 1)
                        nc.vector.tensor_tensor(chunk(hid_lo, 2 * i + t), h[:, :],
                                                chunk(hid_hi, 2 * i + t).bitcast(F32), ALU.subtract).then_inc(h_lo, 1)

                with ve.Fori(0, FC // 2 - 1) as i:
                    body(i)
                body(FC // 2 - 1)

            ffn(0, 1)

            def down0_body(i):
                for u in range(8):
                    if u % 4 == 3:
                        t = u // 4
                        m = 2 * i + t
                        residual(m, t, i * 8 + (U0["down0"] + u + 1))
                        wait(ve, tile_free, i * 2 + (T0["down0"] + t + 1))
                        gain_lo(m, m + 2 * DC, "mix1")
                    prepare(ve, unit_lo, "down0", i, u)

            with ve.Fori(0, 3) as i:
                down0_body(i)
            down0_body(3)

            L0, B0 = U0["latent"], T0["latent"]

            def v_copy(n):
                ve.wait_ge(v_prod, n + 1)
                nc.vector.tensor_copy(v_nat[:, n % TB, (n // TB) * 512:(n // TB + 1) * 512],
                                      ps[:, 4 + n % 3, :]).then_inc(v_out, 1)

            def mean_square(k):
                ve.wait_ge(stat_done, 4 + k)
                if k:
                    ve.wait_ge(root_done, 4)
                nc.vector.tensor_tensor(lat_ms[:, :], ps[:, STAT_BANK, :], inv[:, :], ALU.mult).then_inc(ms_done, 1)
                ve.wait_ge(ms_done, 2 * k + 1)
                nc.vector.tensor_tensor(lat_ms[:, :], lat_ms[:, :], inv[:, :], ALU.mult).then_inc(ms_done, 1)

            def c_q_out(c):
                ve.wait_ge(lat_sq, LC + c + 1)
                nc.vector.tensor_tensor(c_q[:, c, :], ps[:, LC + 1 + c, :], inv[:, :], ALU.mult).then_inc(tile_free, 1)

            def latent_lo(k, g):
                c_ = (c_kv, c_q)[k]
                for c in range(LC):
                    n = LC * k + c
                    ve.wait_ge(lat_hi, n + 1)
                    nc.vector.scalar_tensor_tensor(hid_lo[:, LAT + n, :], c_[:, c, :],
                                                   gain[:, rows[g] + c:rows[g] + c + 1],
                                                   hid_hi[:, LAT + n, :].bitcast(F32), ALU.mult,
                                                   ALU.subtract).then_inc(lat_lo, 1)

            make_inv(ve, 2)
            for c in range(LC):
                prepare(ve, unit_lo, "latent", 0, c)
            mean_square(0)
            make_inv(ve, 3, inv_lat)
            nc.vector.tensor_tensor(inv_lat[:, :], inv_lat[:, :], inv[:, :], ALU.mult).then_inc(inv_both, 1)
            ve.wait_ge(inv_both, 1)
            for c in range(LC):
                nc.vector.tensor_tensor(c_kv[:, c, :], ps[:, c, :], inv_lat[:, :], ALU.mult).then_inc(lat_scaled, 1)
            prepare(ve, unit_lo, "latent", 0, LC)
            latent_lo(0, "kv_norm")
            ve.wait_ge(w_used, L0 + LC + 1)
            ve.wait_ge(tables_in, 32)
            nc.vector.tensor_tensor(k_rope[NOPE:QK, :], ps[NOPE:QK, 2, :], rope[NOPE:QK, :], ALU.mult).then_inc(rope_step, 1)
            nc.vector.tensor_tensor(rope_s[NOPE:QK, :], ps[QK:P, 2, :], rope[QK:P, :], ALU.mult).then_inc(tile_free, LC + 1)
            c_q_out(0)
            prepare(ve, unit_lo, "latent", 0, LC + 1)
            ve.wait_ge(rope_step, 1)
            ve.wait_ge(tile_free, B0 + LC + 1)
            nc.vector.tensor_tensor(k_rope[NOPE:QK, :], k_rope[NOPE:QK, :], rope_s[NOPE:QK, :], ALU.add).then_inc(rope_step, 1)
            ve.wait_ge(rope_step, 2)
            nc.vector.tensor_tensor(k_rope[NOPE:QK, :], k_rope[NOPE:QK, :], inv[NOPE:QK, :], ALU.mult).then_inc(k_rope_done, 1)
            c_q_out(1)
            prepare(ve, unit_lo, "latent", 0, LC + 2)
            mean_square(1)
            v_copy(0)
            make_inv(ve, 4, inv_lat)
            for c in range(LC):
                nc.vector.tensor_tensor(c_q[:, c, :], c_q[:, c, :], inv_lat[:, :], ALU.mult).then_inc(lat_scaled, 1)
            latent_lo(1, "q_norm")

            for n in range(1, TB):
                v_copy(n)
            for u in range(4):
                prepare(ve, unit_lo, "kv_up", 0, u)

            def rope_q(hd, par):
                wait(ve, q_out, hd + 1)
                wait(ve, q_rope, hd)
                nc.vector.tensor_tensor(rope_s[NOPE:QK, :], q_T[QK:P, par, :], rope[QK:P, :], ALU.mult).then_inc(q_sine, 1)

            def row_max(hd, par):
                wait(ve, p_turned, 3 * (hd - 2) + 3)
                for n, j in enumerate((3, 1, 2, 0)):
                    W = (j + 1) * P
                    if n < 3:
                        wait_apart(ve, s_prod, 3 * hd + (n + 1))
                    bank, col = {3: (0, 0), 1: (2, 0), 2: (1, 0), 0: (1, 384)}[j]
                    ins = nc.vector.tensor_tensor_reduce(
                        prob[:, par, L_OFF[j]:L_OFF[j] + W], ps[:, bank, col:col + W], mask[:, S - W:S],
                        1.0, -3.0e38, ALU.add, ALU.max, mx[:, par, j:j + 1])
                    if n != 2:
                        ins.then_inc(s_read, 1)
                    if n in (1, 3):
                        wait(ve, s_read, 3 * hd + (n + 3) // 2)
                        two = slice(1 - n // 2, 4 - n // 2, 2)
                        nc.vector.tensor_scalar(neg_mx[:, par, two], mx[:, par, two], -SCALE, None,
                                                ALU.mult).then_inc(mx_neg, 1)

            def normalise(hd, par):
                wait(ve, p_ready, hd - 1)
                for n, js in enumerate(((3, 1), (2, 0))):
                    wait(ve, exp_done, 2 * hd + (n + 1))
                    two = slice(js[1], js[0] + 1, 2)
                    nc.vector.reciprocal(rec[:, par, two], sums[:, par, two]).then_inc(rec_done, 1)
                    wait(ve, rec_done, 2 * hd + (n + 1))
                    for j in js:
                        blk = prob[:, par, L_OFF[j]:L_OFF[j] + (j + 1) * P]
                        ins = nc.vector.tensor_scalar(blk, blk, rec[:, par, j:j + 1], None, ALU.mult)
                ins.then_inc(p_ready, 1)

            def head_out(pair):
                wait(ve, o_hi, pair + 1)
                nc.vector.tensor_tensor(chunk(hid_lo, pair), ps[:, 6, :], chunk(hid_hi, pair).bitcast(F32),
                                        ALU.subtract).then_inc(o_lo, 1)

            def attend(i, first=False, ahead=True):
                for par in range(2):
                    if not (first and par == 0):
                        if par == 1 and ahead:
                            rope_q(2 * i + 2, 0)
                        row_max(2 * i + par, par)
                        if par == 0 and ahead:
                            unit_lo(ve, "q_up", i, 0)
                        if par == 0:
                            rope_q(2 * i + 1, 1)
                        if par == 0 and not ahead:
                            unit_lo(ve, "mla_out", 0, 1)
                    if par == 1 and not first:
                        head_out(i - 1)
                    normalise(2 * i + par, par)
                    if isinstance(i, int) and par == 0 and i >= PAIRS - 2:
                        unit_lo(ve, "mla_out", 0, 2 * (i - PAIRS + 2))

            for n in range(2, 4):
                k_rope_part(nc.vector.tensor_copy, n).then_inc(k_rope_late, 1)
            for n in range(TB, 2 * TB):
                v_copy(n)
                if n == TB + 1:
                    rope_q(0, 0)
                if n == TB + 2:
                    rope_q(1, 1)
                    row_max(0, 0)
            attend(0, first=True)
            attend(1)
            with ve.Fori(2, PAIRS - 2) as i:
                attend(i)
            attend(PAIRS - 2)
            attend(PAIRS - 1, ahead=False)
            unit_lo(ve, "mla_out", 0, 3)
            head_out(PAIRS - 1)

            out_body("mla_out", 0, "ffn1", 3)
            out_body("mla_out", 1, "ffn1", 3)
            ffn(1, 5)

            def copy_out(m, bank):
                wait(ve, out_turned, m + 1)
                nc.vector.tensor_copy(o_nat[:, :, ds(m * P, P)],
                                      ps[:, bank, :].rearrange("p (t f) -> p t f", t=TB)).then_inc(out_nat, 1)

            def down1_body(i, first=False, last=False):
                for u in range(8):
                    if u == 2 and not first:
                        copy_out(2 * i - 1, 5)
                    if u == 6:
                        copy_out(2 * i, 4)
                    if u % 4 == 3 and not (last and u == 7):
                        residual(2 * i + u // 4, u // 4, i * 8 + (U0["down1"] + u + 1))
                    prepare(ve, unit_lo, "down1", i, u)

            down1_body(0, first=True)
            with ve.Fori(1, 3) as i:
                down1_body(i)
            down1_body(3, last=True)
            for half in range(2):
                tok = slice(half * S // 2, (half + 1) * S // 2)
                ve.wait_ge(half_done, half + 1)
                nc.vector.tensor_tensor(xT[:, DC - 1, tok], ps[:, 1 + half, 0:S // 2], xT[:, DC - 1, tok],
                                        ALU.add).then_inc(x_last, 1)
                ve.wait_ge(x_last, half + 1)
                nc.vector.tensor_tensor(h[:, tok], xT[:, DC - 1, tok], xT[:, DC - 1, tok], ALU.mult).then_inc(sq_last, 1)
                ve.wait_ge(out_turned, DC + half)
                two = slice(2 * half, 2 * half + 2)
                nc.vector.tensor_copy(o_nat[:, two, (DC - 1) * P:DC * P],
                                      ps[:, 5, tok].rearrange("p (t f) -> p t f", t=2)).then_inc(out_nat, 1)
                ve.wait_ge(root_done, 7 + half)
                nc.vector.reciprocal(inv_c[:, two], root_c[:, two]).then_inc(inv_done, 1)
                ve.wait_ge(inv_done, 7 + half)
                ve.wait_ge(out_nat, DC + half)
                t = 2 * half
                nc.vector.tensor_scalar(o_nat[:, t, :], o_nat[:, t, :], inv_c[:, t:t + 1], None, ALU.mult).then_inc(out_final[0], 1)

        @block.tensor
        def _(pe):
            def turn_x(m):
                if m % 2 == 0:
                    pe.wait_ge(x_in[m // 2], 16)
                if m >= X_BANKS:
                    pe.wait_ge(x_copied, m - X_BANKS + 1)
                for t in range(TB):
                    ins = nc.tensor.transpose(ps[:, X_BANK + m % X_BANKS, t * P:(t + 1) * P],
                                              x_nat[:, t, m * P:(m + 1) * P], ident)
                ins.then_inc(x_turned, 1)

            def turn_gains(n):
                nc.tensor.transpose(ps[:, STAT_BANK, 0:n], gain_rows[0:n, :], ident[0:n, 0:n]).then_inc(gain_turned, 1)

            def keep_warm(n):
                for _ in range(n):
                    nc.tensor.matmul(ps[:, 2, 0:P], ones[:, :], ones[:, :], start=True, stop=True)

            pe.wait_ge(ones_set, 1)
            keep_warm(5)
            pe.wait_ge(ident_in, 16)
            pe.wait_ge(mix_in, 16)
            turn_gains(2 * DC)
            keep_warm(4)
            for m in range(X_BANKS):
                turn_x(m)
                if m == 1:
                    keep_warm(3)

            def wide_phase(name, ready, ready0, norm=None):
                first_two(name, ready, ready0, norm)
                for u in range(2, shape[name][0]):
                    chunk_products(name, 0, u, every, ready, ready0)
                later_bodies(name, ready, ready0)

            def later_bodies(name, ready, ready0):
                with pe.Fori(1, shape[name][1]) as i:
                    for u in range(shape[name][0]):
                        chunk_products(name, i, u, every, ready, ready0)

            def down_tile(name, i, t, turn=None):
                l = int(name[-1])
                for q in range(4):
                    u = 4 * t + q
                    v, s, _, _ = unit_numbers(name, i, u)
                    if q == 0:
                        tile_wait(pe, name, i, t)
                    wait(pe, w_lo, v + 1)
                    c0, n = DOWN[q]
                    for k in range(n):
                        c = c0 + k
                        if t == 0 and (k == 0 or c >= FC - 2):
                            upto = c if c >= FC - 2 else min(c0 + n - 1, FC - 3)
                            pe.wait_ge(h_lo, l * FC + upto + 1)
                        col = slice(k * P, k * P + P)
                        ins = product(ps[:, t, :], wgt_hi[:, s, col], wgt_lo[:, s, col], hid_hi[:, c, :],
                                      hid_lo[:, c, :], c == 0, c == FC - 1)
                    ins.then_inc(w_used, 1)
                    if q == 1 and turn is not None:
                        turn()

            chunk_products("conv_in", 0, 0, every[:2], x_lo, 0)
            turn_x(4)
            turn_x(5)
            chunk_products("conv_in", 0, 0, every[2:4], x_lo, 0)
            turn_x(6)
            chunk_products("conv_in", 0, 1, every[:4], x_lo, 0)
            turn_x(7)
            for k in every[4:]:
                chunk_products("conv_in", 0, 0, [k], x_lo, 0)
                chunk_products("conv_in", 0, 1, [k], x_lo, 0)
            pe.wait_ge(gain_in, 16 * 5)
            pe.wait_ge(gain_ready, 1)
            turn_gains(G_ROWS)
            chunk_products("conv_in", 0, 2, every[:1], x_lo, 0)
            pe.wait_ge(gain_ready, 2)
            pe.wait_ge(sq_added, X_POOL)
            pe.wait_ge(sq_rest, 2)
            pe.wait_ge(x_copied, DC)
            nc.tensor.matmul(ps[:, STAT_BANK, :], ones[:, :], sq_sum[:, :], start=True, stop=False)
            nc.tensor.matmul(ps[:, STAT_BANK, :], ones[:, :], c_r[:, :], start=False, stop=True).then_inc(stat_done, 1)
            chunk_products("conv_in", 0, 2, every[1:], x_lo, 0)
            later_bodies("conv_in", x_lo, 0)
            wide_phase("conv_out", y_lo, 0)
            wide_phase("ffn0", x_lo, DC, norm=1)
            for t in range(2):
                down_tile("down0", 0, t)
            with pe.Fori(1, 4) as i:
                for t in range(2):
                    down_tile("down0", i, t)

            def latent_statistic(k):
                pe.wait_ge(lat_sq, LC * (k + 1))
                pe.wait_ge(root_done, 3)
                if k:
                    pe.wait_ge(ms_done, 2)
                for c in range(LC):
                    ins = nc.tensor.matmul(ps[:, STAT_BANK, :], ones[:, :], lat_square[:, c, :], start=c == 0,
                                           stop=c == LC - 1)
                ins.then_inc(stat_done, 1)

            first_two("latent", x_lo, 2 * DC, norm=2)
            chunk_products("latent", 0, 2, every, x_lo, 2 * DC)
            latent_statistic(0)
            chunk_products("latent", 0, 3, every, x_lo, 2 * DC)
            chunk_products("latent", 0, 4, every, x_lo, 2 * DC)

            def lat(part, n):
                return part[:, LAT + n, :]

            def q_pair(pair, par):
                hd = 2 * pair + par
                wait(pe, q_out, hd)
                if par == 0:
                    wait(pe, w_lo, pair + (U0["q_first"] + 1))
                first = isinstance(pair, int) and pair == 0
                s = shape["q_first" if first else "q_up"][2][0]
                for c in range(LC):
                    col = slice((2 * c + par) * P, (2 * c + par + 1) * P)
                    ins = product(ps[:, 7, :], wgt_hi[:, s, col], wgt_lo[:, s, col], lat(hid_hi, LC + c),
                                  lat(hid_lo, LC + c), c == 0, c == LC - 1)
                ins.then_inc(q_prod, 1)

            def q_used(pair):
                wait(pe, q_prod, 2 * pair + 2)
                pe.sem_inc(w_used, 1)

            def logits(hd, par):
                wait(pe, q_rope, hd + 1)
                for n, js in enumerate(((3,), (1,), (2, 0))):
                    wait(pe, s_read, 3 * (hd - 1) + (n + 1))
                    for j in js:
                        W = (j + 1) * P
                        bank, col = {3: (0, 0), 1: (2, 0), 2: (1, 0), 0: (1, 384)}[j]
                        ins = nc.tensor.matmul(ps[:, bank, col:col + W], q_T[0:QK, par, j * P:(j + 1) * P],
                                               k_T[0:QK, ds(hd, 1), 0:W].rearrange("p a w -> p (a w)"),
                                               start=True, stop=True)
                    ins.then_inc(s_prod, 1)

            n_k, n_v = 0, 0
            for half in range(2):
                units = [U0["kv_up"] + 2 * half + n for n in range(2)]
                slot = plan["slots"][units[0]]
                for pair in range(4):
                    if pair % 2 == 0:
                        pe.wait_ge(w_lo, units[pair // 2] + 1)
                    if n_k == 0:
                        pe.wait_ge(lat_scaled, LC)
                    elif n_k == 2:
                        pe.wait_ge(tile_free, T0["latent"] + LC + 1)
                    elif n_k == 3:
                        pe.wait_ge(tile_free, T0["latent"] + LC + 2)
                    elif n_k >= 4:
                        pe.wait_ge(k_out, n_k - 3)
                    s = slot + pair // 2
                    for c in range(LC):
                        if n_k == 0:
                            pe.wait_ge(lat_lo, c + 1)
                        col = (2 * c + pair % 2) * P
                        wh, wl = (part[:, s, col:col + P] for part in (wgt_hi, wgt_lo))
                        ins = product(ps[:, n_k % 4, :], wh, wl, lat(hid_hi, c), lat(hid_lo, c), c == 0, c == LC - 1)
                    ins.then_inc(k_prod, 1)
                    n_k += 1
                    if n_k == 1:
                        latent_statistic(1)
                for b in range(TB):
                    if half == 1 and b == 2:
                        pe.wait_ge(lat_lo, 2 * LC)
                        pe.wait_ge(ms_done, 4)
                        q_pair(0, 0)
                    if half == 1 and b == 3:
                        q_pair(0, 1)
                        pe.wait_ge(k_out, PAIRS)
                        pe.wait_ge(k_rope_early, 2)
                        pe.wait_ge(k_rope_late, 2)
                        logits(0, 0)
                    if n_v >= 3:
                        pe.wait_ge(v_out, n_v - 2)
                    if n_v == 0:
                        pe.wait_ge(tile_free, T0["latent"] + 5)
                        pe.wait_ge(lat_sq, 2 * LC)
                    tok = slice(b * P, (b + 1) * P)
                    for c in range(LC):
                        vh, vl = (part[:, slot:slot + 2, 512 + c * 256:768 + c * 256] for part in (wgt_hi, wgt_lo))
                        acc = ps[:, 4 + n_v % 3, :].rearrange("p (s n) -> p s n", s=2)
                        nc.tensor.matmul(acc, lat(hid_hi, c)[:, tok], vh, start=c == 0, stop=False)
                        nc.tensor.matmul(acc, lat(hid_hi, c)[:, tok], vl, start=False, stop=False)
                        ins = nc.tensor.matmul(acc, lat(hid_lo, c)[:, tok], vh, start=False, stop=c == LC - 1)
                    ins.then_inc(v_prod, 1)
                    n_v += 1
                pe.wait_ge(v_prod, n_v)
                pe.wait_ge(k_prod, n_k)
                pe.sem_inc(w_used, 2)
            q_used(0)

            def turn(hd, par):
                wait(pe, p_ready, hd + 1)
                wait(pe, pt_ready, hd)
                for bs in ((0,), (2,), (1, 3)):
                    for b in bs:
                        bank, col = {0: (3, 0), 2: (5, 0), 1: (4, 0), 3: (4, 384)}[b]
                        for j in range(b, TB):
                            ins = nc.tensor.transpose(ps[:, bank, col + (j - b) * P:col + (j - b + 1) * P],
                                                      prob[:, par, L_OFF[j] + b * P:L_OFF[j] + (b + 1) * P], ident)
                    ins.then_inc(p_turned, 1)

            def weigh(hd, par, pair):
                wait(pe, pt_ready, hd + 1)
                wait(pe, v_ready, hd + 1)
                if par == 0:
                    wait(pe, o_lo, pair)
                for b in range(TB):
                    n = (TB - b) * P
                    ins = nc.tensor.matmul(ps[VD * par:VD * par + VD, 6, b * P:S], v_head[:, par, b, :],
                                           prob_Ts[par][:, 0, PT_OFF[b]:PT_OFF[b] + n], start=b == 0, stop=b == TB - 1)
                ins.then_inc(pv_done, 1)

            def attend(i, first=False, ahead=True):
                for par in range(2):
                    if not (first and par == 0):
                        logits(2 * i + par, par)
                    if not first:
                        weigh(2 * i + (par - 2), par, i - 1)
                    if ahead:
                        q_pair(i + 1, par)
                    if not (first and par == 0):
                        turn(2 * i + (par - 1), 1 - par)
                if ahead:
                    q_used(i + 1)

            attend(0, first=True)
            attend(1)
            with pe.Fori(2, PAIRS - 1) as i:
                attend(i)
            attend(PAIRS - 1, ahead=False)
            pe.wait_ge(s_read, 3 * HEADS)
            chunk_products("mla_out", 0, 0, early, o_lo, 0)
            weigh(HEADS - 2, 0, PAIRS - 1)
            turn(HEADS - 1, 1)
            chunk_products("mla_out", 0, 1, early, o_lo, 0)
            weigh(HEADS - 1, 1, PAIRS - 1)
            chunk_products("mla_out", 0, 2, early, o_lo, 0)
            for u in range(3):
                chunk_products("mla_out", 0, u, late, o_lo, 0)
            pe.wait_ge(pt_ready, HEADS)
            chunk_products("mla_out", 0, 3, every, o_lo, 0)
            later_bodies("mla_out", o_lo, 0)
            wide_phase("ffn1", x_lo, 3 * DC, norm=3)

            def turn_out(m, buf):
                wait(pe, out_scaled, m + 1)
                wait(pe, out_nat, m)
                for t in range(TB):
                    ins = nc.tensor.transpose(ps[:, 4 + buf, t * P:(t + 1) * P], o_chunk[:, buf, t * P:(t + 1) * P], ident)
                ins.then_inc(out_turned, 1)

            down_tile("down1", 0, 0)
            down_tile("down1", 0, 1, turn=lambda: turn_out(0, 0))
            with pe.Fori(1, 3) as i:
                down_tile("down1", i, 0, turn=lambda: turn_out(2 * i - 1, 1))
                down_tile("down1", i, 1, turn=lambda: turn_out(2 * i, 0))
            down_tile("down1", 3, 0, turn=lambda: turn_out(5, 1))

            def half_out(half):
                pe.wait_ge(out_scaled, DC + half)
                pe.wait_ge(out_nat, DC - 1 + half)
                for t in range(2 * half, 2 * half + 2):
                    ins = nc.tensor.transpose(ps[:, 5, t * P:(t + 1) * P], o_chunk[:, 1, t * P:(t + 1) * P], ident)
                ins.then_inc(out_turned, 1)
                pe.wait_ge(sq_added, squares_before(5) - 1)
                pe.wait_ge(sq_last, half + 1)
                pe.wait_ge(root_done, 6 + half)
                for t in range(2 * half, 2 * half + 2):
                    for part in (sq_sum, h):
                        ins = nc.tensor.matmul(ps[:, STAT_BANK, t:t + 1], part[:, t * P:(t + 1) * P], ones[:, 0:1],
                                               start=part is sq_sum, stop=part is h)
                ins.then_inc(stat_done, 1)

            tile_wait(pe, "down1", 3, 1)
            for half in range(2):
                tok = slice(half * S // 2, (half + 1) * S // 2)
                for q in range(4):
                    v, s, _, _ = unit_numbers("down1", 3, 4 + q)
                    wait(pe, w_lo, v + 1)
                    c0, n = DOWN[q]
                    for k in range(n):
                        c = c0 + k
                        col = slice(k * P, k * P + P)
                        ins = product(ps[:, 1 + half, 0:S // 2], wgt_hi[:, s, col], wgt_lo[:, s, col],
                                      hid_hi[:, c, tok], hid_lo[:, c, tok], c == 0, c == FC - 1)
                    if q == 1 and half == 0:
                        turn_out(DC - 2, 0)
                    if q == 1 and half == 1:
                        half_out(0)
                ins.then_inc(half_done, 1)
            half_out(1)


_INS = ["x", "norm_mix_g", "norm_ffn_g", "ffn_w_gate", "ffn_w_up", "ffn_w_down", "final_norm_g", "conv_w_in",
        "conv_w", "conv_w_out", "mla_w_dq", "mla_q_norm_g", "mla_w_uq", "mla_w_dkv", "mla_kv_norm_g",
        "mla_w_ukv", "mla_w_o"]


def shape_constants(seq, rope_dim, theta=10000.0):
    import numpy as np

    ident = np.eye(P, dtype=np.float32)
    mask = np.zeros((P, seq), np.float32)
    mask[0:P // 2, seq - P // 2:seq] = -1e30
    inv = (np.float32(theta) ** (-np.arange(0, rope_dim, 2, dtype=np.float32) / np.float32(rope_dim))).astype(np.float32)
    ang = inv[:, None] * np.arange(seq, dtype=np.float32)[None, :]
    cos, sin = np.cos(ang), np.sin(ang)
    rope = np.zeros((P, seq), np.float32)
    rope[64:96] = np.concatenate([cos, cos])
    rope[96:128] = np.concatenate([-sin, sin])
    return np.concatenate([ident, mask, rope], axis=1).astype(np.float32)


def kernel(**inputs):
    import numpy as np
    import concourse.bacc as bacc
    from concourse.bass_utils import run_bass_kernel_spmd as run

    nc = bacc.Bacc("TRN2", target_bir_lowering=False, num_devices=1)
    arrays, args = {}, {}
    for name in _INS:
        a = np.ascontiguousarray(inputs[name])
        arrays[f"in_{name}"] = a
        args[name] = nc.dram_tensor(f"in_{name}", a.shape, mybir.dt.from_np(a.dtype), kind="ExternalInput").ap()
    shape = inputs["x"].shape
    table = shape_constants(shape[1], 32)
    arrays["constants"] = table
    consts = nc.dram_tensor("constants", table.shape, F32, kind="ExternalInput").ap()
    out = nc.dram_tensor("out", shape, F32, kind="ExternalOutput").ap()
    trunk_kernel(nc, args, consts, out)
    r = run(nc, [arrays], core_ids=[0])
    return r.results[0]["out"]
```
